# Optimizing a Trainium2 kernel written in Bass

```python
import jax, jax.numpy as jnp
from jax import lax
import numpy as np

D_MODEL = 2048
BATCH = 1
SEQ = 256
DEPTH = 2

CHUNK = 64
N_HEADS = 16
HEAD_DIM = D_MODEL // N_HEADS
D_FF = -(-8 * D_MODEL // (3 * 256)) * 256
N_A = DEPTH // 2
N_B = DEPTH - N_A
Q_BLOCK = 128
EPS = 1e-6

kernel_name = "fox_yoco_stickbreaking_hybrid"

def rmsnorm(x, g):
    xf = x.astype(jnp.float32)
    y = xf * lax.rsqrt(jnp.mean(xf * xf, axis=-1, keepdims=True) + EPS) * g.astype(jnp.float32)
    return y.astype(x.dtype)

def split_heads(t):
    b, s, _ = t.shape
    return t.reshape(b, s, N_HEADS, HEAD_DIM).transpose(0, 2, 1, 3)

def merge_heads(o):
    b, h, s, d = o.shape
    return o.transpose(0, 2, 1, 3).reshape(b, s, h * d)

def to_blocks(t):
    b, h, s, d = t.shape
    return t.reshape(b, h, s // Q_BLOCK, Q_BLOCK, d).transpose(2, 0, 1, 3, 4)

def from_blocks(t):
    nb, b, h, q, d = t.shape
    return t.transpose(1, 2, 0, 3, 4).reshape(b, h, nb * q, d)

def forgetting_attention(q, k, v, log_f):
    b, h, s, _ = q.shape
    nb = s // Q_BLOCK
    c = jnp.cumsum(log_f, axis=-1)
    c_blocks = c.reshape(b, h, nb, Q_BLOCK).transpose(2, 0, 1, 3)
    key_pos = jnp.arange(s)
    scale = HEAD_DIM ** -0.5

    def block(args):
        q_blk, c_blk, i = args
        q_pos = i * Q_BLOCK + jnp.arange(Q_BLOCK)
        logits = jnp.einsum('bhqd,bhkd->bhqk', q_blk, k,
                            preferred_element_type=jnp.float32) * scale
        logits = logits + c_blk[..., :, None] - c[..., None, :]
        mask = key_pos[None, :] <= q_pos[:, None]
        logits = jnp.where(mask, logits, -jnp.inf)
        p = jax.nn.softmax(logits, axis=-1)
        return jnp.einsum('bhqk,bhkd->bhqd', p.astype(v.dtype), v)

    out = lax.map(block, (to_blocks(q), c_blocks, jnp.arange(nb)))
    return from_blocks(out)

def stick_breaking_attention(q, k, v):
    s = q.shape[2]
    nb = s // Q_BLOCK
    key_pos = jnp.arange(s)
    scale = HEAD_DIM ** -0.5

    def block(args):
        q_blk, i = args
        q_pos = i * Q_BLOCK + jnp.arange(Q_BLOCK)
        z = jnp.einsum('bhqd,bhkd->bhqk', q_blk, k,
                       preferred_element_type=jnp.float32) * scale
        mask = key_pos[None, :] < q_pos[:, None]
        log_beta = jax.nn.log_sigmoid(z)
        log_1m = jnp.where(mask, jax.nn.log_sigmoid(-z), 0.0)
        suffix = lax.cumsum(log_1m, axis=3, reverse=True) - log_1m
        weights = jnp.where(mask, jnp.exp(log_beta + suffix), 0.0)
        return jnp.einsum('bhqk,bhkd->bhqd', weights.astype(v.dtype), v)

    out = lax.map(block, (to_blocks(q), jnp.arange(nb)))
    return from_blocks(out)

def swiglu(x, w_gate, w_up, w_down):
    return (jax.nn.silu(x @ w_gate) * (x @ w_up)) @ w_down

def setup_inputs(seed: int = 0) -> dict:
    key = jax.random.key(seed)
    ks = jax.random.split(key, 16)
    d = D_MODEL
    f32 = jnp.float32
    nrm = lambda k, shape, fan_in: jax.random.normal(k, shape, f32) * (fan_in ** -0.5)
    return {
        "x": jax.random.normal(ks[0], (BATCH, SEQ, d), f32),
        "attn_norm": 1.0 + 0.02 * jax.random.normal(ks[1], (DEPTH, d), f32),
        "ffn_norm": 1.0 + 0.02 * jax.random.normal(ks[2], (DEPTH, d), f32),
        "a_w_in": nrm(ks[3], (N_A, d, 3 * d + N_HEADS), d),
        "a_b_f": 3.0 + 0.5 * jax.random.normal(ks[4], (N_A, N_HEADS), f32),
        "a_w_out": nrm(ks[5], (N_A, d, d), d),
        "kv_norm": 1.0 + 0.02 * jax.random.normal(ks[6], (d,), f32),
        "w_kv": nrm(ks[7], (d, 2 * d), d),
        "b_w_q": nrm(ks[8], (N_B, d, d), d),
        "b_w_out": nrm(ks[9], (N_B, d, d), d),
        "ffn_w_gate": nrm(ks[10], (DEPTH, d, D_FF), d),
        "ffn_w_up": nrm(ks[11], (DEPTH, d, D_FF), d),
        "ffn_w_down": nrm(ks[12], (DEPTH, D_FF, d), D_FF),
        "final_norm": 1.0 + 0.02 * jax.random.normal(ks[13], (d,), f32),
    }

def reference(x, attn_norm, ffn_norm, a_w_in, a_b_f, a_w_out, kv_norm, w_kv,
              b_w_q, b_w_out, ffn_w_gate, ffn_w_up, ffn_w_down, final_norm):
    d = D_MODEL
    h = x
    k_shared = None
    v_shared = None
    for layer in range(DEPTH):
        hn = rmsnorm(h, attn_norm[layer])
        if layer < N_A:
            proj = hn @ a_w_in[layer]
            q = split_heads(proj[..., :d])
            k = split_heads(proj[..., d:2 * d])
            v = split_heads(proj[..., 2 * d:3 * d])
            f_logit = proj[..., 3 * d:].astype(jnp.float32) + a_b_f[layer].astype(jnp.float32)
            log_f = jax.nn.log_sigmoid(f_logit).transpose(0, 2, 1)
            o = forgetting_attention(q, k, v, log_f)
            h = h + merge_heads(o) @ a_w_out[layer]
        else:
            j = layer - N_A
            q = split_heads(hn @ b_w_q[j])
            o = stick_breaking_attention(q, k_shared, v_shared)
            h = h + merge_heads(o) @ b_w_out[j]
        h = h + swiglu(rmsnorm(h, ffn_norm[layer]), ffn_w_gate[layer],
                       ffn_w_up[layer], ffn_w_down[layer])
        if layer == N_A - 1:
            kv = rmsnorm(h, kv_norm) @ w_kv
            k_shared = split_heads(kv[..., :d])
            v_shared = split_heads(kv[..., d:])
    return rmsnorm(h, final_norm)


_drawn_inputs = setup_inputs


def setup_inputs(seed=0):
    import zlib

    import numpy as np

    out = dict(_drawn_inputs(seed))
    spreads = {}
    factors = {'attn_norm': 4.209, 'ffn_norm': 2.878, 'kv_norm': 4.977, 'final_norm': 2.779}
    for name, (base, spread) in spreads.items():
        noise = np.random.default_rng([zlib.crc32(name.encode()), seed]).standard_normal(out[name].shape)
        drawn = base * np.exp(spread * noise) if base else spread * noise
        out[name] = __import__('jax').numpy.asarray(drawn.astype(out[name].dtype))
    for name, factor in factors.items():
        out[name] = (out[name] * factor).astype(out[name].dtype)
    return out
```

```python
from contextlib import ExitStack

import concourse.bass as bass
from concourse import mybir

F32 = mybir.dt.float32
F32R = mybir.dt.float32r
BF16 = mybir.dt.bfloat16
ALU = mybir.AluOpType
ACT = mybir.ActivationFunctionType
AX_X = mybir.AxisListType.X

P = 128
COLS = 512
KT = 4
RAW = 4
SPLIT = 2
AHEAD = 2
HEADS_G = 4
MASKED = -1e30
EPS = 1e-6


def build(nc, x, attn_norm, ffn_norm, a_w_in, a_b_f, a_w_out, kv_norm, w_kv, b_w_q, b_w_out,
          ffn_w_gate, ffn_w_up, ffn_w_down, final_norm, out):
    _, S, D = x.shape
    NH = a_b_f.shape[1]
    DH = D // NH
    FF = ffn_w_gate.shape[2]
    T = S // P
    KD = D // P
    KF = FF // P
    SCALE = float(DH) ** -0.5
    assert (S, DH, COLS) == (2 * P, P, HEADS_G * DH) and D == 4 * COLS and attn_norm.shape[0] == 2

    NG = NH // HEADS_G
    KG = KD // KT
    NF = FF // COLS
    ND = D // COLS
    DOWN = [KT] * 8 + [3] * 4
    assert sum(DOWN) == KF and len(DOWN) % RAW == 0 and KG % RAW == 0
    QKV_STEPS = 3 * KG
    STEPS = NG * QKV_STEPS + ND * KG + NF * 2 * KG + ND * len(DOWN)
    BLOCKS = 3 * NG + ND + 2 * NF + ND
    at_out = NG * QKV_STEPS
    at_ffn = at_out + ND * KG
    at_down = at_ffn + NF * 2 * KG
    OUT_ORDER = [(0, 0), (0, 1), (0, 2), (1, 0), (1, 1), (1, 2), (0, 3), (1, 3)] + \
                [(b, k) for b in range(2, ND) for k in range(KG)]
    TJ_OUT = [ND, 2 * ND + NF + ND + KG]
    TJ_FFN = [TJ_OUT[0] + ND, TJ_OUT[1] + ND]
    TJ_DOWN = TJ_FFN[0] + NF
    TJ_Q = TJ_DOWN + ND
    assert TJ_Q + KG == TJ_OUT[1]

    FIRST_STAGE = 2 * KG + 1

    def stages(step):
        todo = []
        for stage in (3, 2, 1, 0):
            for back in (0, 1):
                j = step + back * QKV_STEPS - FIRST_STAGE - stage
                if 0 <= j < HEADS_G:
                    todo.append((stage, j, back))
        return todo

    with ExitStack() as ctx:
        def sb(name, shape, dt, where=None):
            return (where or ctx).enter_context(nc.sbuf_tensor(name, shape, dt))

        def sem(name):
            return ctx.enter_context(nc.semaphore(name))

        res = sb("res", [P, T, D], F32)
        xT = sb("xT", [P, KD, 2, S], F32R)
        raw = sb("raw", [P, RAW, KT, COLS], F32)
        w_hi = sb("w_hi", [P, SPLIT, KT, COLS], F32R)
        w_lo = sb("w_lo", [P, SPLIT, KT, COLS], F32R)
        mix = sb("mix", [P, T, COLS], F32)
        ident = sb("ident", [P, P], F32)
        ident_b = sb("ident_b", [P, P], BF16)
        mask_q = sb("mask_q", [P, P], BF16)
        mask_k = sb("mask_k", [P, P], BF16)
        neg_prefix = sb("neg_prefix", [P, P], F32)
        neg_suffix = sb("neg_suffix", [P, P], F32)
        neg_ones = sb("neg_ones", [P, P], F32)
        gains = sb("gains", [P, 5, KD], F32)
        sums = sb("sums", [P, 5, T, ND], F32)
        ssq = sb("ssq", [P, 5, T], F32)
        meansq = sb("meansq", [P, 5, T], F32)
        neg_half = sb("neg_half", [P, T], F32)
        rstd = sb("rstd", [P, 5, T], F32)
        row_max = sb("row_max", [P, T], F32)
        neg_max = sb("neg_max", [P, T], F32)
        row_sum = sb("row_sum", [P, T], F32)
        row_inv = sb("row_inv", [P, T], F32)

        with ExitStack() as region:
            oT = sb("oT", [P, NH, 2, S], F32R, region)
            kn = sb("kn", [P, T, COLS], F32, region)
            vn = sb("vn", [P, T, COLS], F32, region)
            qkT = sb("qkT", [P, 2, S], F32, region)
            work0 = sb("work0", [P, 3 * P], F32, region)
            work1 = sb("work1", [P, 3 * P], F32, region)
            probsT = sb("probsT", [P, 3 * P], F32, region)
            with ExitStack() as fox:
                neg_c = sb("neg_c", [P, NH, S], F32, fox)
                gain_rows = sb("gain_rows", [5 * KD, P], F32, fox)
                f_raw = sb("f_raw", [P, KD, NH], F32, fox)
                f_hi = sb("f_hi", [P, KD, NH], F32R, fox)
                f_lo = sb("f_lo", [P, KD, NH], F32R, fox)
                f_bias = sb("f_bias", [P, NH], F32, fox)
                f_logit = sb("f_logit", [P, T, NH], F32, fox)
                f_abs = sb("f_abs", [P, T, NH], F32, fox)
                f_exp = sb("f_exp", [P, T, NH], F32, fox)
                f_log1p = sb("f_log1p", [P, T, NH], F32, fox)
                log_f = sb("log_f", [P, T, NH], F32, fox)
                c_tok = sb("c_tok", [P, T, NH], F32, fox)
                c_row = sb("c_row", [NH, S], F32, fox)
            with ExitStack() as stick:
                xqT = sb("xqT", [P, KD, 2, S], F32R, stick)
        hid = sb("hid", [P, KF, 2, S], F32R)

        c_dram = nc.dram_tensor("c_rows", [NH, S], F32, kind="Internal").ap()

        acc = [[ctx.enter_context(nc.psum_tensor(f"acc{a}{t}", [P, COLS], F32)) for t in range(T)]
               for a in range(2)]
        tr = [ctx.enter_context(nc.psum_tensor(f"tr{a}", [P, COLS], F32)) for a in range(2)]
        ps_s = ctx.enter_context(nc.psum_tensor("ps_s", [P, COLS], F32))
        ps_o = ctx.enter_context(nc.psum_tensor("ps_o", [P, COLS], F32))
        ps_z = [ps_s, tr[1]]

        x_loaded = [sem(f"x_loaded{b}") for b in range(ND)]
        gains_loaded = sem("gains_loaded")
        f_loaded = sem("f_loaded")
        bias_loaded = sem("bias_loaded")
        consts_cleared = sem("consts_cleared")
        consts_ready = sem("consts_ready")
        gains_turned = sem("gains_turned")
        gains_ready = sem("gains_ready")
        raw_loaded = [sem(f"raw_loaded{i}") for i in range(RAW)]
        hi_ready = sem("hi_ready")
        lo_ready = sem("lo_ready")
        slab_done = sem("slab_done")
        acc0_ready = sem("acc0_ready")
        acc_free = sem("acc_free")
        sig_ready = sem("sig_ready")
        turned = sem("turned")
        turned_hi = sem("turned_hi")
        turned_lo = sem("turned_lo")
        squares_ready = sem("squares_ready")
        pool_step = sem("pool_step")
        rstd_ready = sem("rstd_ready")
        f_split_hi = sem("f_split_hi")
        f_split_lo = sem("f_split_lo")
        f_summed = sem("f_summed")
        f_step = sem("f_step")
        f_act = sem("f_act")
        c_summed = sem("c_summed")
        c_copied = sem("c_copied")
        c_stored = sem("c_stored")
        neg_c_loaded = sem("neg_c_loaded")
        res_copied = sem("res_copied")
        qk_turned = sem("qk_turned")
        qk_copied = sem("qk_copied")
        scored = sem("scored")
        shifted = sem("shifted")
        max_found = sem("max_found")
        max_negated = sem("max_negated")
        exp_ready = sem("exp_ready")
        log_ready = sem("log_ready")
        inv_ready = sem("inv_ready")
        probs_ready = sem("probs_ready")
        probs_turned = sem("probs_turned")
        probsT_ready = sem("probsT_ready")
        head_summed = sem("head_summed")
        head_hi = sem("head_hi")
        head_ready = sem("head_ready")
        out_ready = sem("out_ready")
        out_stored = sem("out_stored")

        def tiles(w):
            return w.rearrange("(k p) n -> p k n", p=P)

        x_t = x[0].rearrange("(t p) d -> p t d", p=P)
        out_t = out[0].rearrange("(t p) d -> p t d", p=P)
        win_t = tiles(a_w_in[0])
        wkv_t = tiles(w_kv)
        wq_t = tiles(b_w_q[0])
        wout_t = [tiles(a_w_out[0]), tiles(b_w_out[0])]
        gate_t = [tiles(ffn_w_gate[layer]) for layer in range(2)]
        up_t = [tiles(ffn_w_up[layer]) for layer in range(2)]
        down_t = [tiles(ffn_w_down[layer]) for layer in range(2)]

        QKV_KINDS = ["qkv", "kqv"]

        def qkv_source(layer, kind):
            if layer == 0:
                return win_t, "qkv".index(kind) * D
            return (wq_t, 0) if kind == "q" else (wkv_t, "kv".index(kind) * D)

        def cols(i):
            return slice(i * COLS, (i + 1) * COLS)

        def of(i, n=COLS):
            return bass.ds(i * n, n)

        block = ctx.enter_context(nc.Block())

        @block.sync
        def _(sp):
            def load(s, slot, src, kts):
                if not (isinstance(s, int) and s < RAW):
                    sp.wait_ge(lo_ready, s - RAW + 1)
                sp.dma_start(raw[:, slot % RAW, 0:kts, :], src).then_inc(raw_loaded[slot % RAW], 16)

            for b in range(ND):
                sp.dma_start(res[:, :, cols(b)], x_t[:, :, cols(b)]).then_inc(x_loaded[b], 16)

            def qkv_group(layer, g):
                for step in range(QKV_STEPS):
                    src, at = qkv_source(layer, QKV_KINDS[layer][step // KG])
                    k0 = step % KG * KT
                    load(layer * STEPS + g * QKV_STEPS + step, step,
                         src[:, k0:k0 + KT, bass.ds(g * COLS + at, COLS)], KT)

            def ffn_block(layer, j):
                for step in range(2 * KG):
                    src = (gate_t, up_t)[step // KG][layer]
                    k0 = step % KG * KT
                    load(layer * STEPS + at_ffn + j * 2 * KG + step, step,
                         src[:, k0:k0 + KT, of(j)], KT)

            def down_block(layer, b):
                k0 = 0
                for step, kts in enumerate(DOWN):
                    load(layer * STEPS + at_down + b * len(DOWN) + step, step,
                         down_t[layer][:, k0:k0 + kts, of(b)], kts)
                    k0 += kts

            for layer in range(2):
                qkv_group(layer, 0)
                with sp.Fori(1, NG) as g:
                    qkv_group(layer, g)
                for i, (b, k) in enumerate(OUT_ORDER):
                    load(layer * STEPS + at_out + i, i, wout_t[layer][:, k * KT:(k + 1) * KT, cols(b)], KT)
                with sp.Fori(0, NF) as j:
                    ffn_block(layer, j)
                with sp.Fori(0, ND) as b:
                    down_block(layer, b)

            sp.wait_ge(lo_ready, 2 * STEPS - RAW + 1)
            sp.dma_start(raw[:, 0, :, :].rearrange("p k n -> p (k n)"),
                         final_norm.partition_broadcast(P)).then_inc(raw_loaded[0], 16)
            for b in range(ND):
                sp.wait_ge(out_ready, T * (b + 1))
                sp.dma_start(out_t[:, :, cols(b)], res[:, :, cols(b)]).then_inc(out_stored, 16)
            sp.wait_ge(out_stored, 16 * ND)

        @block.gpsimd
        def _(pool):
            pool.memset(ident[:], 0.0).then_inc(consts_cleared, 1)
            pool.memset(ident_b[:], 0.0).then_inc(consts_cleared, 1)
            pool.memset(mask_q[:], 0.0).then_inc(consts_cleared, 1)
            pool.memset(mask_k[:], 0.0).then_inc(consts_cleared, 1)
            pool.memset(neg_prefix[:], -1.0).then_inc(consts_cleared, 1)
            pool.memset(neg_suffix[:], -1.0).then_inc(consts_cleared, 1)
            pool.memset(neg_ones[:], -1.0).then_inc(consts_cleared, 1)
            pool.memset(neg_half[:], -0.5).then_inc(consts_cleared, 1)
            pool.wait_ge(consts_cleared, 8)

            def select(t, compare, fill, base, row, col):
                pool.affine_select(out=t[:], in_=t[:], compare_op=compare, fill=fill, base=base,
                                   pattern=[[col, P]], channel_multiplier=row).then_inc(consts_ready, 1)

            select(ident, ALU.not_equal, 1.0, 0, 1, -1)
            select(ident_b, ALU.not_equal, 1.0, 0, 1, -1)
            select(mask_q, ALU.is_ge, MASKED, 0, 1, -1)
            select(mask_k, ALU.is_ge, MASKED, -1, -1, 1)
            select(neg_prefix, ALU.is_ge, 0.0, 0, -1, 1)
            select(neg_suffix, ALU.is_ge, 0.0, 0, 1, -1)

            def norm(n):
                pool.wait_ge(squares_ready, (n + 1) * ND * T)
                for b in range(1, ND):
                    if b > 1:
                        pool.wait_ge(pool_step, ND * n + b - 1)
                    left = sums[:, n, :, 0] if b == 1 else ssq[:, n, :]
                    pool.tensor_tensor(ssq[:, n, :], left, sums[:, n, :, b], ALU.add).then_inc(pool_step, 1)
                pool.wait_ge(pool_step, ND * n + ND - 1)
                pool.tensor_scalar(meansq[:, n, :], ssq[:, n, :], 1.0 / D, EPS, ALU.mult, ALU.add)\
                    .then_inc(pool_step, 1)
                pool.wait_ge(pool_step, ND * n + ND)
                pool.tensor_tensor(rstd[:, n, :], meansq[:, n, :], neg_half[:], ALU.pow).then_inc(rstd_ready, 1)

            norm(0)
            pool.wait_ge(c_copied, 2)
            pool.dma_start(c_dram, c_row[:, :]).then_inc(c_stored, 16)
            pool.wait_ge(c_stored, 16)
            pool.dma_start(neg_c[:, :, :].rearrange("p h s -> p (h s)"),
                           c_dram.rearrange("h s -> (h s)").partition_broadcast(P)).then_inc(neg_c_loaded, 16)
            for n in range(1, 5):
                norm(n)

        @block.scalar
        def _(act):
            def split_hi(s, slot, kts=KT):
                act.wait_ge(raw_loaded[slot % RAW], raw_uses(s, slot))
                if not (isinstance(s, int) and s < SPLIT):
                    act.wait_ge(slab_done, s - SPLIT + 1)
                act.activation(w_hi[:, slot % SPLIT, 0:kts, :], raw[:, slot % RAW, 0:kts, :], ACT.Copy)\
                    .then_inc(hi_ready, 1)

            def raw_uses(s, slot):
                return 16 // RAW * (s - slot % RAW) + 16

            def turn_hi(n, dst, k0, gain=None):
                for a in range(2):
                    act.wait_ge(turned, 2 * n + a + 1)
                    if gain is None:
                        last = act.activation(dst[:, bass.ds(k0 + 2 * a, 2), 0, :],
                                              tr[a][:, :].rearrange("p (k s) -> p k s", k=2), ACT.Copy)
                    else:
                        for i in range(2):
                            last = act.activation(dst[:, k0 + 2 * a + i, 0, :], tr[a][:, of(i, S)],
                                                  ACT.Copy, scale=gains[:, gain, bass.ds(k0 + 2 * a + i, 1)])
                    last.then_inc(turned_hi, 1)

            def squares(n, b):
                for t in range(T):
                    act.activation(mix[:, t, 0:COLS // 2].bitcast(BF16), res[:, t, of(b)], ACT.Square,
                                   accum_out=sums[:, n, t, bass.ds(b, 1)]).then_inc(squares_ready, 1)

            def stage(layer, number, j, g):
                n = layer * NH + g * HEADS_G + j
                if number == 0:
                    act.wait_ge(qk_turned, n + 1)
                    act.activation(qkT[:, :, :].rearrange("p a s -> p (a s)"), tr[0][:, :], ACT.Copy)\
                        .then_inc(qk_copied, 1)
                elif number == 1 and layer == 0:
                    act.wait_ge(max_negated, n + 1)
                    for t, (a, b) in enumerate(((0, P), (P, 3 * P))):
                        last = act.activation(work1[:, a:b], work0[:, a:b], ACT.Exp, bias=neg_max[:, t:t + 1],
                                              accum_out=row_sum[:, t:t + 1])
                    last.then_inc(exp_ready, 1)
                elif number == 1:
                    act.wait_ge(scored, n + 1)
                    act.activation(work0[:, :], ps_z[j % 2][:, 0:3 * P], ACT.Abs).then_inc(shifted, 1)
                    act.wait_ge(shifted, n + 1)
                    act.activation(work1[:, :], work0[:, :], ACT.Exp, scale=-1.0).then_inc(exp_ready, 1)
                    act.wait_ge(exp_ready, n + 1)
                    act.activation(work0[:, :], work1[:, :], ACT.Ln, bias=1.0).then_inc(log_ready, 1)
                elif number == 2:
                    act.wait_ge(probs_turned, n + 1)
                    if layer == 0:
                        act.activation(probsT[:, :], tr[1][:, 0:3 * P], ACT.Copy).then_inc(probsT_ready, 1)
                    else:
                        act.activation(probsT[:, :], ps_z[j % 2][:, 0:3 * P], ACT.Exp).then_inc(probsT_ready, 1)
                elif number == 3:
                    act.wait_ge(head_summed, n + 1)
                    act.activation(oT[:, g * HEADS_G + j, 0, :], ps_o[:, 0:S], ACT.Copy).then_inc(head_hi, 1)

            for i, g in enumerate((attn_norm[0], ffn_norm[0], kv_norm, attn_norm[1], ffn_norm[1])):
                act.dma_start(gain_rows[i * KD:(i + 1) * KD, :], g.rearrange("(k p) -> k p", p=P))\
                    .then_inc(gains_loaded, 16)
            act.dma_start(f_raw[:, :, :], win_t[:, :, 3 * D:3 * D + NH]).then_inc(f_loaded, 16)
            act.dma_start(f_bias[:, :], a_b_f[0].partition_broadcast(P)).then_inc(bias_loaded, 16)
            act.wait_ge(gains_turned, 1)
            act.activation(gains[:, :, :].rearrange("p a k -> p (a k)"), tr[0][:, 0:5 * KD], ACT.Copy)\
                .then_inc(gains_ready, 1)
            act.wait_ge(gains_ready, 1)
            turn_hi(0, xT, 0, 0)
            split_hi(0, 0)
            turn_hi(1, xT, KT, 0)
            split_hi(1, 1)
            turn_hi(2, xT, 2 * KT, 0)
            act.wait_ge(f_loaded, 16)
            act.activation(f_hi[:, :, :], f_raw[:, :, :], ACT.Copy).then_inc(f_split_hi, 1)
            for b in range(ND):
                if b > 0:
                    act.wait_ge(squares_ready, b * T)
                squares(0, b)
                if b == ND - 2:
                    act.wait_ge(x_loaded[ND - 1], 16)

            def qkv_group(layer, g, first):
                for step in range(QKV_STEPS):
                    s = layer * STEPS + g * QKV_STEPS + step
                    split_hi(s + AHEAD, step + AHEAD)
                    if first and step == 1:
                        turn_hi(ND - 1 if layer == 0 else TJ_DOWN + ND - 1, xT, (ND - 1) * KT, 2 * layer)
                    if first and layer == 1 and 2 <= step < 2 + KG:
                        turn_hi(TJ_Q + step - 2, xqT, (step - 2) * KT, 3)
                    if first and layer == 0 and step == KG - 1:
                        act.wait_ge(f_step, 1)
                        act.activation(f_abs[:, :, :], f_logit[:, :, :], ACT.Abs).then_inc(f_act, 1)
                        act.wait_ge(f_act, 1)
                        act.activation(f_exp[:, :, :], f_abs[:, :, :], ACT.Exp, scale=-1.0).then_inc(f_act, 1)
                        act.wait_ge(f_act, 2)
                        act.activation(f_log1p[:, :, :], f_exp[:, :, :], ACT.Ln, bias=1.0).then_inc(f_act, 1)
                    for number, j, back in stages(step):
                        if not (first and back):
                            stage(layer, number, j, g - back)

            for layer in range(2):
                qkv_group(layer, 0, True)
                with act.Fori(1, NG) as g:
                    qkv_group(layer, g, False)

                for i, (b, k) in enumerate(OUT_ORDER):
                    s = layer * STEPS + at_out + i
                    split_hi(s + AHEAD, i + AHEAD)
                    for number, j, back in stages(i):
                        if back:
                            stage(layer, number, j, NG - 1)
                    if k == KG - 1:
                        act.wait_ge(acc_free, 2 * (layer * BLOCKS + 3 * NG + b + 1))
                        act.wait_ge(squares_ready, ((1 + 2 * layer) * ND + b) * T)
                        squares(1 + 2 * layer, b)
                    turn = OUT_TURNS.get(i)
                    if turn is not None:
                        turn_hi(TJ_OUT[layer] + turn, xT, turn * KT, 1 + 3 * layer)

                def ffn_block(j, first):
                    for step in range(2 * KG):
                        s = layer * STEPS + at_ffn + j * 2 * KG + step
                        blk = layer * BLOCKS + 3 * NG + ND + 2 * j
                        if step == KG - 1:
                            if first:
                                act.wait_ge(rstd_ready, 2 + 2 * layer)
                            for t in range(T):
                                if t == 0:
                                    act.wait_ge(acc0_ready, blk + 1)
                                else:
                                    act.wait_ge(slab_done, s + 1)
                                act.activation(mix[:, t, :], acc[(1 + layer) % 2][t][:, :], ACT.Sigmoid,
                                               scale=rstd[:, 1 + 2 * layer, t:t + 1]).then_inc(sig_ready, 1)
                        split_hi(s + AHEAD, step + AHEAD)
                        if step == 1:
                            if first:
                                turn_hi(TJ_OUT[layer] + ND - 1, xT, (ND - 1) * KT, 1 + 3 * layer)
                            else:
                                turn_hi(TJ_FFN[layer] + j - 1, hid, (j - 1) * KT)

                ffn_block(0, True)
                with act.Fori(1, NF) as j:
                    ffn_block(j, False)

                def down_block(b, first=False, last=False):
                    for step in range(len(DOWN)):
                        s = layer * STEPS + at_down + b * len(DOWN) + step
                        if step == len(DOWN) - 1:
                            act.wait_ge(acc_free, 2 * (layer * BLOCKS + BLOCKS - ND + b + 1))
                            act.wait_ge(squares_ready, ((2 + 2 * layer) * ND + b) * T)
                            squares(2 + 2 * layer, b)
                            if layer == 0:
                                act.wait_ge(squares_ready, (2 * ND + b + 1) * T)
                        if not (last and step + AHEAD >= len(DOWN)):
                            split_hi(s + AHEAD, step + AHEAD, DOWN[(step + AHEAD) % len(DOWN)])
                        if step == 1 and first:
                            turn_hi(TJ_FFN[layer] + NF - 1, hid, (NF - 1) * KT)
                        elif step == 1 and layer == 0:
                            turn_hi(TJ_DOWN + b - 1, xT, (b - 1) * KT, 2)
                        if step == len(DOWN) - 1 and layer == 0:
                            for t in range(T):
                                copy = act.activation(mix[:, t, :], res[:, t, of(b)], ACT.Copy)
                            copy.then_inc(res_copied, 1)

                down_block(0, first=True)
                if layer == 0:
                    with act.Fori(1, ND) as b:
                        down_block(b)
                else:
                    with act.Fori(1, ND - 1) as b:
                        down_block(b)
                    down_block(ND - 1, last=True)

        @block.vector
        def _(dve):
            def split_lo(s, slot, kts=KT):
                dve.wait_ge(hi_ready, s + 1)
                dve.tensor_tensor(w_lo[:, slot % SPLIT, 0:kts, :], raw[:, slot % RAW, 0:kts, :],
                                  w_hi[:, slot % SPLIT, 0:kts, :].bitcast(F32), ALU.subtract)\
                    .then_inc(lo_ready, 1)

            def turn_lo(n, dst, k0, gain=None):
                for a in range(2):
                    dve.wait_ge(turned_hi, 2 * n + a + 1)
                    if gain is None:
                        last = dve.tensor_tensor(dst[:, bass.ds(k0 + 2 * a, 2), 1, :],
                                                 tr[a][:, :].rearrange("p (k s) -> p k s", k=2),
                                                 dst[:, bass.ds(k0 + 2 * a, 2), 0, :].bitcast(F32), ALU.subtract)
                    else:
                        for i in range(2):
                            k = k0 + 2 * a + i
                            last = dve.scalar_tensor_tensor(
                                out=dst[:, k, 1, :], in0=tr[a][:, of(i, S)], scalar=gains[:, gain, bass.ds(k, 1)],
                                in1=dst[:, k, 0, :].bitcast(F32), op0=ALU.mult, op1=ALU.subtract)
                    last.then_inc(turned_lo, 1)

            def tile_summed(t, blk, s):
                if t == 0:
                    dve.wait_ge(acc0_ready, blk + 1)
                else:
                    dve.wait_ge(slab_done, s + 1)

            def take_qkv(layer, kind, blk, s, bank):
                for t in range(T):
                    tile_summed(t, blk, s)
                    dst = {"q": mix, "k": kn, "v": vn}[kind]
                    dve.tensor_scalar(dst[:, t, :], bank[t][:, :], rstd[:, 2 * layer, t:t + 1],
                                      SCALE if kind == "q" else None, ALU.mult,
                                      *([ALU.mult] if kind == "q" else [])).then_inc(acc_free, 1)

            def take_residual(b, blk, s, bank):
                for t in range(T):
                    tile_summed(t, blk, s)
                    dve.tensor_tensor(res[:, t, of(b)], res[:, t, of(b)], bank[t][:, :], ALU.add)\
                        .then_inc(acc_free, 1)

            def early(layer, number, j, g):
                n = layer * NH + g * HEADS_G + j
                h = g * HEADS_G + j
                if number == 1 and layer == 0:
                    dve.wait_ge(scored, n + 1)
                    for t, (a, b) in enumerate(((0, P), (P, 3 * P))):
                        last = dve.scalar_tensor_tensor(
                            out=work0[:, a:b], in0=ps_s[:, a:b], scalar=c_tok[:, t, bass.ds(h, 1)],
                            in1=neg_c[:, h, 0:b - a], op0=ALU.add, op1=ALU.add)
                    last.then_inc(shifted, 1)
                    dve.wait_ge(shifted, n + 1)
                    for t, (a, b) in enumerate(((0, P), (P, 3 * P))):
                        last = dve.tensor_reduce(row_max[:, t:t + 1], work0[:, a:b], AX_X, ALU.max)
                    last.then_inc(max_found, 1)
                    dve.wait_ge(max_found, n + 1)
                    dve.tensor_scalar(neg_max[:, :], row_max[:, :], -1.0, None, ALU.mult)\
                        .then_inc(max_negated, 1)

            def late(layer, number, j, g):
                n = layer * NH + g * HEADS_G + j
                if number == 1 and layer == 0:
                    dve.wait_ge(exp_ready, n + 1)
                    dve.reciprocal(row_inv[:, :], row_sum[:, :]).then_inc(inv_ready, 1)
                    dve.wait_ge(inv_ready, n + 1)
                    for t, (a, b) in enumerate(((0, P), (P, 3 * P))):
                        last = dve.tensor_scalar(work1[:, a:b], work1[:, a:b], row_inv[:, t:t + 1], None, ALU.mult)
                    last.then_inc(probs_ready, 1)
                elif number == 1:
                    dve.wait_ge(log_ready, n - NH + 1)
                    dve.scalar_tensor_tensor(out=work1[:, :], in0=ps_z[j % 2][:, 0:3 * P], scalar=0.0,
                                             in1=work0[:, :], op0=ALU.max, op1=ALU.add).then_inc(probs_ready, 1)
                elif number == 3:
                    dve.wait_ge(head_hi, n + 1)
                    dve.tensor_tensor(oT[:, g * HEADS_G + j, 1, :], ps_o[:, 0:S],
                                      oT[:, g * HEADS_G + j, 0, :].bitcast(F32), ALU.subtract)\
                        .then_inc(head_ready, 1)

            dve.wait_ge(gains_ready, 1)
            turn_lo(0, xT, 0, 0)
            split_lo(0, 0)
            turn_lo(1, xT, KT, 0)
            split_lo(1, 1)
            turn_lo(2, xT, 2 * KT, 0)
            dve.wait_ge(f_split_hi, 1)
            dve.tensor_tensor(f_lo[:, :, :], f_raw[:, :, :], f_hi[:, :, :].bitcast(F32), ALU.subtract)\
                .then_inc(f_split_lo, 1)

            def qkv_group(layer, g, first):
                for step in range(QKV_STEPS):
                    s = layer * STEPS + g * QKV_STEPS + step
                    which = step // KG
                    if step % KG == KG - 1:
                        if first and step == KG - 1:
                            dve.wait_ge(rstd_ready, 1 + 2 * layer)
                        take_qkv(layer, QKV_KINDS[layer][which], layer * BLOCKS + 3 * g + which, s,
                                 acc[(which + layer) % 2])
                    if first and layer == 0 and step == KG - 1:
                        dve.wait_ge(f_summed, 1)
                        dve.wait_ge(bias_loaded, 16)
                        for t in range(T):
                            last = dve.scalar_tensor_tensor(
                                out=f_logit[:, t, :], in0=ps_s[:, of(t, NH)], scalar=rstd[:, 0, t:t + 1],
                                in1=f_bias[:, :], op0=ALU.mult, op1=ALU.add)
                        last.then_inc(f_step, 1)
                    if first and layer == 0 and step == KG + 1:
                        dve.wait_ge(c_summed, 1)
                        dve.tensor_scalar(c_tok[:, :, :].rearrange("p t h -> p (t h)"), ps_s[:, 0:T * NH],
                                          -1.0, None, ALU.mult).then_inc(c_copied, 1)
                        dve.tensor_copy(c_row[:, :], ps_o[0:NH, 0:S]).then_inc(c_copied, 1)
                    if first and layer == 0 and step == FIRST_STAGE + 1:
                        dve.wait_ge(neg_c_loaded, 16)
                        dve.wait_ge(c_copied, 2)
                    todo = [(number, j, back) for number, j, back in stages(step) if not (first and back)]
                    for number, j, back in todo:
                        early(layer, number, j, g - back)
                    split_lo(s + AHEAD, step + AHEAD)
                    if first and step == 1:
                        turn_lo(ND - 1 if layer == 0 else TJ_DOWN + ND - 1, xT, (ND - 1) * KT, 2 * layer)
                    if first and layer == 1 and 2 <= step < 2 + KG:
                        turn_lo(TJ_Q + step - 2, xqT, (step - 2) * KT, 3)
                    if first and layer == 0 and step == KG - 1:
                        dve.wait_ge(f_act, 3)
                        dve.scalar_tensor_tensor(out=log_f[:, :, :], in0=f_logit[:, :, :], scalar=0.0,
                                                 in1=f_log1p[:, :, :], op0=ALU.min, op1=ALU.subtract)\
                            .then_inc(f_step, 1)
                    for number, j, back in todo:
                        late(layer, number, j, g - back)

            for layer in range(2):
                qkv_group(layer, 0, True)
                with dve.Fori(1, NG) as g:
                    qkv_group(layer, g, False)

                for i, (b, k) in enumerate(OUT_ORDER):
                    s = layer * STEPS + at_out + i
                    if k == KG - 1:
                        take_residual(b, layer * BLOCKS + 3 * NG + b, s, acc[(1 + b + layer) % 2])
                    todo = [(number, j) for number, j, back in stages(i) if back]
                    for number, j in todo:
                        early(layer, number, j, NG - 1)
                    split_lo(s + AHEAD, i + AHEAD)
                    for number, j in todo:
                        late(layer, number, j, NG - 1)
                    turn = OUT_TURNS.get(i)
                    if turn is not None:
                        turn_lo(TJ_OUT[layer] + turn, xT, turn * KT, 1 + 3 * layer)

                def ffn_block(j, first):
                    for step in range(2 * KG):
                        s = layer * STEPS + at_ffn + j * 2 * KG + step
                        blk = layer * BLOCKS + 3 * NG + ND + 2 * j
                        if step == KG - 1:
                            if first:
                                dve.wait_ge(rstd_ready, 2 + 2 * layer)
                            for t in range(T):
                                dve.wait_ge(sig_ready, T * (layer * NF + j) + t + 1)
                                dve.scalar_tensor_tensor(
                                    out=mix[:, t, :], in0=acc[(1 + layer) % 2][t][:, :],
                                    scalar=rstd[:, 1 + 2 * layer, t:t + 1], in1=mix[:, t, :],
                                    op0=ALU.mult, op1=ALU.mult).then_inc(acc_free, 1)
                        if step == 2 * KG - 1:
                            dve.wait_ge(acc_free, 2 * (blk + 1))
                            for t in range(T):
                                tile_summed(t, blk + 1, s)
                                dve.scalar_tensor_tensor(
                                    out=mix[:, t, :], in0=acc[layer % 2][t][:, :],
                                    scalar=rstd[:, 1 + 2 * layer, t:t + 1], in1=mix[:, t, :],
                                    op0=ALU.mult, op1=ALU.mult).then_inc(acc_free, 1)
                        split_lo(s + AHEAD, step + AHEAD)
                        if step == 1:
                            if first:
                                turn_lo(TJ_OUT[layer] + ND - 1, xT, (ND - 1) * KT, 1 + 3 * layer)
                            else:
                                turn_lo(TJ_FFN[layer] + j - 1, hid, (j - 1) * KT)

                ffn_block(0, True)
                with dve.Fori(1, NF) as j:
                    ffn_block(j, False)

                def down_block(b, first=False, last=False):
                    for step in range(len(DOWN)):
                        s = layer * STEPS + at_down + b * len(DOWN) + step
                        if step == len(DOWN) - 1:
                            take_residual(b, layer * BLOCKS + BLOCKS - ND + b, s,
                                          acc[(1 + layer) % 2 if first else layer % 2])
                        if not (last and step + AHEAD >= len(DOWN)):
                            split_lo(s + AHEAD, step + AHEAD, DOWN[(step + AHEAD) % len(DOWN)])
                        if step == 1 and first:
                            turn_lo(TJ_FFN[layer] + NF - 1, hid, (NF - 1) * KT)
                        elif step == 1 and layer == 0:
                            turn_lo(TJ_DOWN + b - 1, xT, (b - 1) * KT, 2)

                down_block(0, first=True)
                if layer == 0:
                    with dve.Fori(1, ND) as b:
                        down_block(b)
                else:
                    with dve.Fori(1, ND - 1) as b:
                        down_block(b)
                    down_block(ND - 1, last=True)

            dve.wait_ge(rstd_ready, 5)
            dve.wait_ge(raw_loaded[0], 16 * (2 * STEPS // RAW + 1))
            dve.wait_ge(acc_free, 4 * BLOCKS)
            for b in range(ND):
                for t in range(T):
                    dve.scalar_tensor_tensor(out=res[:, t, cols(b)], in0=res[:, t, cols(b)],
                                             scalar=rstd[:, 4, t:t + 1], in1=raw[:, 0, b, :],
                                             op0=ALU.mult, op1=ALU.mult).then_inc(out_ready, 1)

        @block.tensor
        def _(pe):
            def slab(s, slot, kts, stat, k0, bank, first, last, blk, back=2):
                pe.wait_ge(lo_ready, s + 1)
                for t in range(T):
                    if first and not (isinstance(blk, int) and blk < back):
                        pe.wait_ge(acc_free, 2 * (blk - back) + t + 1)
                    for k in range(kts):
                        for part, w in ((0, w_hi), (0, w_lo), (1, w_hi)):
                            mm = pe.matmul(bank[t][:, :], stat[:, k0 + k, part, t * P:(t + 1) * P],
                                           w[:, slot % SPLIT, k, :],
                                           start=(first and k == 0 and part == 0 and w is w_hi),
                                           stop=(last and k == kts - 1 and part == 1))
                    if t == 0 and last:
                        mm.then_inc(acc0_ready, 1)
                mm.then_inc(slab_done, 1)

            def turn(n, src, b):
                for a in range(2):
                    if n_past_first(n):
                        pe.wait_ge(turned_lo, 2 * n + a - 1)
                    for i in range(2):
                        for t in range(T):
                            mm = pe.transpose(tr[a][:, i * S + t * P:i * S + (t + 1) * P],
                                              src(t, b, 2 * a + i), ident[:, :])
                    mm.then_inc(turned, 1)

            def n_past_first(n):
                return not (isinstance(n, int) and n == 0)

            def from_res(t, b, i):
                return res[:, t, b * COLS + i * P:b * COLS + (i + 1) * P]

            def from_mix(t, b, i):
                return mix[:, t, i * P:(i + 1) * P]

            def stage(layer, number, j, g):
                n = layer * NH + g * HEADS_G + j
                head = slice(j * DH, (j + 1) * DH)
                if number == 0:
                    if j == 0:
                        pe.wait_ge(acc_free, 2 * (layer * BLOCKS + 3 * g + 2))
                    for a, src in enumerate((mix, kn)):
                        for t in range(T):
                            mm = pe.transpose(tr[0][:, a * S + t * P:a * S + (t + 1) * P],
                                              src[:, t, head], ident[:, :])
                    mm.then_inc(qk_turned, 1)
                elif number == 1 and layer == 0:
                    pe.wait_ge(qk_copied, n + 1)
                    for t, (a, b) in enumerate(((0, P), (P, 3 * P))):
                        pe.matmul(ps_s[:, a:b], qkT[:, 0, t * P:(t + 1) * P], qkT[:, 1, 0:b - a],
                                  start=True, stop=False)
                        mm = pe.matmul(ps_s[:, b - P:b], ident_b[:, :], mask_q[:, :], start=False, stop=True)
                    mm.then_inc(scored, 1)
                elif number == 1:
                    z = ps_z[j % 2]
                    pe.wait_ge(qk_copied, n + 1)
                    pe.matmul(z[:, 0:S], qkT[:, 1, 0:P], qkT[:, 0, 0:S], start=True, stop=False,
                              skip_group_check=True)
                    pe.matmul(z[:, 0:P], ident_b[:, :], mask_k[:, :], start=False, stop=False,
                              skip_group_check=True)
                    pe.matmul(z[:, S:S + P], qkT[:, 1, P:S], qkT[:, 0, P:S], start=False, stop=False,
                              skip_group_check=True)
                    mm = pe.matmul(z[:, S:S + P], ident_b[:, :], mask_k[:, :], start=False, stop=True,
                                   skip_group_check=True)
                    mm.then_inc(scored, 1)
                elif number == 2 and layer == 0:
                    pe.wait_ge(probs_ready, n + 1)
                    for i in range(3):
                        mm = pe.transpose(tr[1][:, i * P:(i + 1) * P], work1[:, i * P:(i + 1) * P], ident[:, :])
                    mm.then_inc(probs_turned, 1)
                elif number == 2:
                    z = ps_z[j % 2]
                    pe.wait_ge(probs_ready, n + 1)
                    pe.matmul(z[:, 0:S], neg_suffix[:, :], work1[:, 0:S], start=False, stop=False,
                              skip_group_check=True)
                    pe.matmul(z[:, P:S], neg_ones[:, :], work1[:, S:S + P], start=False, stop=False,
                              skip_group_check=True)
                    mm = pe.matmul(z[:, S:S + P], neg_suffix[:, :], work1[:, S:S + P], start=False, stop=True,
                                   skip_group_check=True)
                    mm.then_inc(probs_turned, 1)
                else:
                    if j == 0:
                        pe.wait_ge(acc_free, 2 * (layer * BLOCKS + 3 * g + 3))
                    if not (isinstance(n, int) and n == 0):
                        pe.wait_ge(head_ready, n)
                    pe.wait_ge(probsT_ready, n + 1)
                    pe.matmul(ps_o[:, 0:S], vn[:, 0, head], probsT[:, 0:S], start=True, stop=False)
                    mm = pe.matmul(ps_o[:, P:S], vn[:, 1, head], probsT[:, S:S + P], start=False, stop=True)
                    mm.then_inc(head_summed, 1)

            pe.wait_ge(consts_ready, 6)
            pe.wait_ge(gains_loaded, 16 * 5)
            pe.transpose(tr[0][:, 0:5 * KD], gain_rows[:, :], ident[0:5 * KD, 0:5 * KD]).then_inc(gains_turned, 1)
            pe.wait_ge(gains_ready, 1)
            for b in range(2):
                pe.wait_ge(x_loaded[b], 16)
                turn(b, from_res, b)

            def qkv_group(layer, g, first):
                for step in range(QKV_STEPS):
                    s = layer * STEPS + g * QKV_STEPS + step
                    which, k = divmod(step, KG)
                    kind = QKV_KINDS[layer][which]
                    stat = xqT if layer == 1 and kind == "q" else xT
                    if first and which == 0:
                        pe.wait_ge(turned_lo, 2 * ((TJ_DOWN if layer else 0) + k + 1))
                    if first and stat is xqT:
                        pe.wait_ge(turned_lo, 2 * (TJ_Q + k + 1))
                    slab(s, step, KT, stat, k * KT, acc[(which + layer) % 2], k == 0, k == KG - 1,
                         layer * BLOCKS + 3 * g + which, 1 if which == 0 and not first else 2)
                    if first and layer == 0 and step < 2:
                        pe.wait_ge(x_loaded[step + 2], 16)
                        turn(step + 2, from_res, step + 2)
                    if first and layer == 1 and step == 1:
                        pe.wait_ge(acc_free, 2 * BLOCKS)
                        turn(TJ_DOWN + ND - 1, from_res, ND - 1)
                    if first and layer == 1 and 2 <= step < 2 + KG:
                        turn(TJ_Q + step - 2, from_res, step - 2)
                    if first and layer == 0 and step == KG - 1:
                        pe.wait_ge(f_split_lo, 1)
                        for t in range(T):
                            for kt in range(KD):
                                for part, w in ((0, f_hi), (0, f_lo), (1, f_hi)):
                                    mm = pe.matmul(ps_s[:, t * NH:(t + 1) * NH], xT[:, kt, part, t * P:(t + 1) * P],
                                                   w[:, kt, :], start=(kt == 0 and part == 0 and w is f_hi),
                                                   stop=(kt == KD - 1 and part == 1))
                        mm.then_inc(f_summed, 1)
                    if first and layer == 0 and step == KG + 1:
                        pe.wait_ge(f_step, 2)
                        pe.matmul(ps_s[:, 0:NH], neg_prefix[:, :], log_f[:, 0, :], start=True, stop=True)
                        pe.matmul(ps_s[:, NH:2 * NH], neg_ones[:, :], log_f[:, 0, :], start=True, stop=False)
                        pe.matmul(ps_s[:, NH:2 * NH], neg_prefix[:, :], log_f[:, 1, :], start=False, stop=True)
                        pe.matmul(ps_o[0:NH, 0:P], log_f[:, 0, :], neg_prefix[:, :], start=True, stop=True)
                        pe.matmul(ps_o[0:NH, P:S], log_f[:, 0, :], neg_ones[:, :], start=True, stop=False)
                        mm = pe.matmul(ps_o[0:NH, P:S], log_f[:, 1, :], neg_prefix[:, :], start=False, stop=True)
                        mm.then_inc(c_summed, 1)
                    if first and layer == 0 and step == FIRST_STAGE:
                        pe.wait_ge(c_copied, 2)
                    for number, j, back in stages(step):
                        if not (first and back):
                            stage(layer, number, j, g - back)

            for layer in range(2):
                qkv_group(layer, 0, True)
                with pe.Fori(1, NG) as g:
                    qkv_group(layer, g, False)

                for i, (b, k) in enumerate(OUT_ORDER):
                    pe.wait_ge(head_ready, layer * NH + HEADS_G * (k + 1))
                    slab(layer * STEPS + at_out + i, i, KT, oT, k * KT, acc[(1 + b + layer) % 2], k == 0,
                         k == KG - 1, layer * BLOCKS + 3 * NG + b)
                    for number, j, back in stages(i):
                        if back:
                            stage(layer, number, j, NG - 1)
                    t = OUT_TURNS.get(i)
                    if t is not None:
                        pe.wait_ge(acc_free, 2 * (layer * BLOCKS + 3 * NG + t + 1))
                        turn(TJ_OUT[layer] + t, from_res, t)

                def ffn_block(j, first):
                    for step in range(2 * KG):
                        which, k = divmod(step, KG)
                        blk = layer * BLOCKS + 3 * NG + ND + 2 * j
                        if first and which == 0:
                            pe.wait_ge(turned_lo, 2 * (TJ_OUT[layer] + k + 1))
                        slab(layer * STEPS + at_ffn + j * 2 * KG + step, step, KT, xT, k * KT,
                             acc[(1 + which + layer) % 2], k == 0, k == KG - 1, blk + which)
                        if step == 1:
                            pe.wait_ge(acc_free, 2 * blk)
                            if first:
                                turn(TJ_OUT[layer] + ND - 1, from_res, ND - 1)
                            else:
                                turn(TJ_FFN[layer] + j - 1, from_mix, 0)

                ffn_block(0, True)
                with pe.Fori(1, NF) as j:
                    ffn_block(j, False)

                def down_block(b, first=False):
                    k0 = 0
                    blk = layer * BLOCKS + BLOCKS - ND + b
                    for step, kts in enumerate(DOWN):
                        if first:
                            pe.wait_ge(turned_lo, 2 * (TJ_FFN[layer] + (k0 + kts - 1) // KT + 1))
                        slab(layer * STEPS + at_down + b * len(DOWN) + step, step, kts, hid, k0,
                             acc[(1 + layer) % 2 if first else layer % 2], step == 0, step == len(DOWN) - 1,
                             blk, 2 if first else 1)
                        k0 += kts
                        if step == 1 and first:
                            pe.wait_ge(acc_free, 2 * blk)
                            turn(TJ_FFN[layer] + NF - 1, from_mix, 0)
                        elif step == 1 and layer == 0:
                            pe.wait_ge(res_copied, b)
                            turn(TJ_DOWN + b - 1, from_mix, 0)

                down_block(0, first=True)
                with pe.Fori(1, ND) as b:
                    down_block(b)


OUT_TURNS = {8: 0, 9: 1, 13: 2}


_INS = ["x", "attn_norm", "ffn_norm", "a_w_in", "a_b_f", "a_w_out", "kv_norm", "w_kv", "b_w_q", "b_w_out",
        "ffn_w_gate", "ffn_w_up", "ffn_w_down", "final_norm"]


def kernel(**inputs):
    import numpy as _np
    import concourse.bacc as _bacc
    from concourse import mybir as _mybir
    from concourse.bass_utils import run_bass_kernel_spmd as _run

    nc = _bacc.Bacc("TRN2", target_bir_lowering=False, num_devices=1)
    arrays, args = {}, []
    for name in _INS:
        a = _np.ascontiguousarray(inputs[name])
        arrays[f"in_{name}_dram"] = a
        args.append(nc.dram_tensor(f"in_{name}_dram", a.shape, _mybir.dt.from_np(a.dtype), kind="ExternalInput").ap())
    shape = inputs["x"].shape
    args.append(nc.dram_tensor("out_0_dram", shape, _mybir.dt.float32, kind="ExternalOutput").ap())
    build(nc, *args)
    r = _run(nc, [arrays], core_ids=[0])
    return r.results[0]["out_0_dram"]
```

```python
from contextlib import ExitStack

import concourse.bass as bass
from concourse import mybir

F32 = mybir.dt.float32
F32R = mybir.dt.float32r
BF16 = mybir.dt.bfloat16
ALU = mybir.AluOpType
ACT = mybir.ActivationFunctionType
AX_X = mybir.AxisListType.X

P = 128
COLS = 512
KT = 4
RAW = 4
SPLIT = 2
AHEAD = 2
HEADS_G = 4
MASKED = -1e30
EPS = 1e-6


def build(nc, x, attn_norm, ffn_norm, a_w_in, a_b_f, a_w_out, kv_norm, w_kv, b_w_q, b_w_out,
          ffn_w_gate, ffn_w_up, ffn_w_down, final_norm, out):
    _, S, D = x.shape
    NH = a_b_f.shape[1]
    DH = D // NH
    FF = ffn_w_gate.shape[2]
    T = S // P
    KD = D // P
    KF = FF // P
    SCALE = float(DH) ** -0.5
    assert (S, DH, COLS) == (2 * P, P, HEADS_G * DH) and D == 4 * COLS and attn_norm.shape[0] == 2

    NG = NH // HEADS_G
    KG = KD // KT
    NF = FF // COLS
    ND = D // COLS
    DOWN = [KT] * 2 + [3] * 4 + [KT] * 6
    assert sum(DOWN) == KF and len(DOWN) % RAW == 0 and KG % RAW == 0
    QKV_STEPS = 3 * KG
    STEPS = NG * QKV_STEPS + ND * KG + NF * 2 * KG + ND * len(DOWN)
    BLOCKS = 3 * NG + ND + 2 * NF + ND
    at_out = NG * QKV_STEPS
    at_ffn = at_out + ND * KG
    at_down = at_ffn + NF * 2 * KG
    OUT_ORDER = [(0, 0), (0, 1), (0, 2), (1, 0), (1, 1), (1, 2), (0, 3), (1, 3)] + \
                [(b, k) for b in range(2, ND) for k in range(KG)]
    TJ_OUT = [ND, 2 * ND + NF + ND + KG]
    TJ_FFN = [TJ_OUT[0] + ND, TJ_OUT[1] + ND]
    TJ_DOWN = TJ_FFN[0] + NF
    TJ_Q = TJ_DOWN + ND
    assert TJ_Q + KG == TJ_OUT[1]

    FIRST_STAGE = 2 * KG + 1

    def stages(step):
        todo = []
        for stage in (3, 2, 1, 0):
            for back in (0, 1):
                j = step + back * QKV_STEPS - FIRST_STAGE - stage
                if 0 <= j < HEADS_G:
                    todo.append((stage, j, back))
        return todo

    with ExitStack() as ctx:
        def sb(name, shape, dt, where=None):
            return (where or ctx).enter_context(nc.sbuf_tensor(name, shape, dt))

        def sem(name):
            return ctx.enter_context(nc.semaphore(name))

        res = sb("res", [P, T, D], F32)
        with ExitStack() as last:
            final_gain = sb("final_gain", [P, D], F32, last)
        xT = sb("xT", [P, KD, 2, S], F32R)
        raw = sb("raw", [P, RAW, KT, COLS], F32)
        w_hi = sb("w_hi", [P, SPLIT, KT, COLS], F32R)
        w_lo = sb("w_lo", [P, SPLIT, KT, COLS], F32R)
        mix = sb("mix", [P, T, COLS], F32)
        ident = sb("ident", [P, P], F32)
        ident_b = sb("ident_b", [P, P], BF16)
        mask_q = sb("mask_q", [P, P], BF16)
        mask_k = sb("mask_k", [P, P], BF16)
        neg_prefix = sb("neg_prefix", [P, P], F32)
        neg_suffix = sb("neg_suffix", [P, P], F32)
        neg_ones = sb("neg_ones", [P, P], F32)
        gains = sb("gains", [P, 5, KD], F32)
        sums = sb("sums", [P, 5, T, ND], F32)
        ssq = sb("ssq", [P, 5, T], F32)
        meansq = sb("meansq", [P, 5, T], F32)
        neg_half = sb("neg_half", [P, T], F32)
        rstd = sb("rstd", [P, 5, T], F32)
        row_max = sb("row_max", [P, T], F32)
        neg_max = sb("neg_max", [P, T], F32)
        row_sum = sb("row_sum", [P, T], F32)
        row_inv = sb("row_inv", [P, T], F32)

        with ExitStack() as region:
            oT = sb("oT", [P, NH, 2, S], F32R, region)
            kn = sb("kn", [P, T, COLS], F32, region)
            vn = sb("vn", [P, T, COLS], F32, region)
            qkT = sb("qkT", [P, 2, S], F32, region)
            work0 = sb("work0", [P, 3 * P], F32, region)
            work1 = sb("work1", [P, 3 * P], F32, region)
            probsT = sb("probsT", [P, 3 * P], F32, region)
            with ExitStack() as fox:
                neg_c = sb("neg_c", [P, NH, S], F32, fox)
                attn_rows = sb("attn_rows", [2 * KD, P], F32, fox)
                gain_rows = sb("gain_rows", [3 * KD, P], F32, fox)
                f_raw = sb("f_raw", [P, KD, NH], F32, fox)
                f_w = sb("f_w", [P, KD, 2, NH], F32R, fox)
                f_bias = sb("f_bias", [P, NH], F32, fox)
                f_part = sb("f_part", [P, T, NH], F32, fox)
                f_logit = sb("f_logit", [P, T, NH], F32, fox)
                f_abs = sb("f_abs", [P, T, NH], F32, fox)
                f_exp = sb("f_exp", [P, T, NH], F32, fox)
                f_log1p = sb("f_log1p", [P, T, NH], F32, fox)
                log_f = sb("log_f", [P, T, NH], F32, fox)
                c_tok = sb("c_tok", [P, T, NH], F32, fox)
                c_row = sb("c_row", [NH, S], F32, fox)
            with ExitStack() as stick:
                xqT = sb("xqT", [P, KD, 2, S], F32R, stick)
        hid = sb("hid", [P, KF, 2, S], F32R)

        c_dram = nc.dram_tensor("c_rows", [NH, S], F32, kind="Internal").ap()

        acc = [[ctx.enter_context(nc.psum_tensor(f"acc{a}{t}", [P, COLS], F32)) for t in range(T)]
               for a in range(2)]
        tr = [ctx.enter_context(nc.psum_tensor(f"tr{a}", [P, COLS], F32)) for a in range(2)]
        ps_s = ctx.enter_context(nc.psum_tensor("ps_s", [P, COLS], F32))
        ps_o = ctx.enter_context(nc.psum_tensor("ps_o", [P, COLS], F32))
        ps_z = [ps_s, tr[1]]

        x_loaded = [sem(f"x_loaded{b}") for b in range(ND)]
        attn_loaded = sem("attn_loaded")
        gains_loaded = sem("gains_loaded")
        f_loaded = sem("f_loaded")
        bias_loaded = sem("bias_loaded")
        ident_cleared = sem("ident_cleared")
        ident_ready = sem("ident_ready")
        consts_cleared = sem("consts_cleared")
        consts_ready = sem("consts_ready")
        gain_loaded = sem("gain_loaded")
        gained = sem("gained")
        gains_turned = sem("gains_turned")
        gains_ready = sem("gains_ready")
        raw_loaded = [sem(f"raw_loaded{i}") for i in range(RAW)]
        hi_ready = sem("hi_ready")
        lo_ready = sem("lo_ready")
        slab_done = sem("slab_done")
        acc0_ready = sem("acc0_ready")
        acc_free = sem("acc_free")
        sig_ready = sem("sig_ready")
        turned = sem("turned")
        turned_hi = sem("turned_hi")
        turned_lo = sem("turned_lo")
        squares_ready = sem("squares_ready")
        pool_step = sem("pool_step")
        rstd_ready = sem("rstd_ready")
        f_split_hi = sem("f_split_hi")
        f_split_lo = sem("f_split_lo")
        f_summed = sem("f_summed")
        f_step = sem("f_step")
        f_act = sem("f_act")
        c_summed = sem("c_summed")
        c_copied = sem("c_copied")
        c_stored = sem("c_stored")
        neg_c_loaded = sem("neg_c_loaded")
        res_copied = sem("res_copied")
        qk_turned = sem("qk_turned")
        qk_copied = sem("qk_copied")
        scored = sem("scored")
        shifted = sem("shifted")
        max_found = sem("max_found")
        max_negated = sem("max_negated")
        exp_ready = sem("exp_ready")
        log_ready = sem("log_ready")
        inv_ready = sem("inv_ready")
        probs_ready = sem("probs_ready")
        probs_turned = sem("probs_turned")
        probsT_ready = sem("probsT_ready")
        head_summed = sem("head_summed")
        head_hi = sem("head_hi")
        head_ready = sem("head_ready")
        out_ready = sem("out_ready")
        out_stored = sem("out_stored")

        def tiles(w):
            return w.rearrange("(k p) n -> p k n", p=P)

        x_t = x[0].rearrange("(t p) d -> p t d", p=P)
        out_t = out[0].rearrange("(t p) d -> p t d", p=P)
        win_t = tiles(a_w_in[0])
        wkv_t = tiles(w_kv)
        wq_t = tiles(b_w_q[0])
        wout_t = [tiles(a_w_out[0]), tiles(b_w_out[0])]
        gate_t = [tiles(ffn_w_gate[layer]) for layer in range(2)]
        up_t = [tiles(ffn_w_up[layer]) for layer in range(2)]
        down_t = [tiles(ffn_w_down[layer]) for layer in range(2)]

        QKV_KINDS = ["qkv", "kqv"]

        def qkv_source(layer, kind):
            if layer == 0:
                return win_t, "qkv".index(kind) * D
            return (wq_t, 0) if kind == "q" else (wkv_t, "kv".index(kind) * D)

        ATTN, FFN, KV = (0, 1), (2, 3), 4

        def cols(i):
            return slice(i * COLS, (i + 1) * COLS)

        def of(i, n=COLS):
            return bass.ds(i * n, n)

        block = ctx.enter_context(nc.Block())

        @block.sync
        def _(sp):
            def load(s, slot, src, kts):
                if not (isinstance(s, int) and s < RAW):
                    sp.wait_ge(lo_ready, s - RAW + 1)
                sp.dma_start(raw[:, slot % RAW, 0:kts, :], src).then_inc(raw_loaded[slot % RAW], 16)

            def load_x(b):
                sp.dma_start(res[:, :, cols(b)], x_t[:, :, cols(b)]).then_inc(x_loaded[b], 16)

            load_x(0)
            load_x(1)

            def qkv_group(layer, g):
                for step in range(QKV_STEPS):
                    if isinstance(g, int) and layer == 0 and step in (1, 2):
                        load_x(step + 1)
                    src, at = qkv_source(layer, QKV_KINDS[layer][step // KG])
                    k0 = step % KG * KT
                    load(layer * STEPS + g * QKV_STEPS + step, step,
                         src[:, k0:k0 + KT, bass.ds(g * COLS + at, COLS)], KT)

            def ffn_block(layer, j):
                for step in range(2 * KG):
                    src = (gate_t, up_t)[step // KG][layer]
                    k0 = step % KG * KT
                    load(layer * STEPS + at_ffn + j * 2 * KG + step, step,
                         src[:, k0:k0 + KT, of(j)], KT)

            def down_block(layer, b):
                k0 = 0
                for step, kts in enumerate(DOWN):
                    load(layer * STEPS + at_down + b * len(DOWN) + step, step,
                         down_t[layer][:, k0:k0 + kts, of(b)], kts)
                    k0 += kts

            for layer in range(2):
                qkv_group(layer, 0)
                with sp.Fori(1, NG) as g:
                    qkv_group(layer, g)
                for i, (b, k) in enumerate(OUT_ORDER):
                    load(layer * STEPS + at_out + i, i, wout_t[layer][:, k * KT:(k + 1) * KT, cols(b)], KT)
                with sp.Fori(0, NF) as j:
                    ffn_block(layer, j)
                down_block(layer, 0)
                if layer == 1:
                    sp.wait_ge(slab_done, STEPS + at_down)
                    sp.dma_start(final_gain[:, :], final_norm.partition_broadcast(P)).then_inc(gain_loaded, 16)
                with sp.Fori(1, ND) as b:
                    down_block(layer, b)

            for b in range(ND):
                sp.wait_ge(out_ready, T * (b + 1))
                sp.dma_start(out_t[:, :, cols(b)], res[:, :, cols(b)]).then_inc(out_stored, 16)
            sp.wait_ge(out_stored, 16 * ND)

        @block.gpsimd
        def _(pool):
            pool.memset(ident[:], 0.0).then_inc(ident_cleared, 1)
            pool.wait_ge(ident_cleared, 1)
            pool.affine_select(out=ident[:], in_=ident[:], compare_op=ALU.not_equal, fill=1.0, base=0,
                               pattern=[[-1, P]], channel_multiplier=1).then_inc(ident_ready, 1)
            pool.memset(ident_b[:], 0.0).then_inc(consts_cleared, 1)
            pool.memset(mask_q[:], 0.0).then_inc(consts_cleared, 1)
            pool.memset(mask_k[:], 0.0).then_inc(consts_cleared, 1)
            pool.memset(neg_prefix[:], -1.0).then_inc(consts_cleared, 1)
            pool.memset(neg_suffix[:], -1.0).then_inc(consts_cleared, 1)
            pool.memset(neg_ones[:], -1.0).then_inc(consts_cleared, 1)
            pool.memset(neg_half[:], -0.5).then_inc(consts_cleared, 1)
            pool.wait_ge(consts_cleared, 7)

            def select(t, compare, fill, base, row, col):
                pool.affine_select(out=t[:], in_=t[:], compare_op=compare, fill=fill, base=base,
                                   pattern=[[col, P]], channel_multiplier=row).then_inc(consts_ready, 1)

            select(ident_b, ALU.not_equal, 1.0, 0, 1, -1)
            select(mask_q, ALU.is_ge, MASKED, 0, 1, -1)
            select(mask_k, ALU.is_ge, MASKED, -1, -1, 1)
            select(neg_prefix, ALU.is_ge, 0.0, 0, -1, 1)
            select(neg_suffix, ALU.is_ge, 0.0, 0, 1, -1)

            def norm(n):
                for b in range(1, ND):
                    pool.wait_ge(squares_ready, (n * ND + b + 1) * T)
                    if b > 1:
                        pool.wait_ge(pool_step, ND * n + b - 1)
                    left = sums[:, n, :, 0] if b == 1 else ssq[:, n, :]
                    pool.tensor_tensor(ssq[:, n, :], left, sums[:, n, :, b], ALU.add).then_inc(pool_step, 1)
                pool.wait_ge(pool_step, ND * n + ND - 1)
                pool.tensor_scalar(meansq[:, n, :], ssq[:, n, :], 1.0 / D, EPS, ALU.mult, ALU.add)\
                    .then_inc(pool_step, 1)
                pool.wait_ge(pool_step, ND * n + ND)
                pool.tensor_tensor(rstd[:, n, :], meansq[:, n, :], neg_half[:], ALU.pow).then_inc(rstd_ready, 1)

            norm(0)
            pool.wait_ge(c_copied, 2)
            pool.dma_start(c_dram, c_row[:, :]).then_inc(c_stored, 16)
            pool.wait_ge(c_stored, 16)
            pool.dma_start(neg_c[:, :, :].rearrange("p h s -> p (h s)"),
                           c_dram.rearrange("h s -> (h s)").partition_broadcast(P)).then_inc(neg_c_loaded, 16)
            for n in range(1, 5):
                norm(n)

        @block.scalar
        def _(act):
            def split_hi(s, slot, kts=KT):
                act.wait_ge(raw_loaded[slot % RAW], raw_uses(s, slot))
                if not (isinstance(s, int) and s < SPLIT):
                    act.wait_ge(slab_done, s - SPLIT + 1)
                act.activation(w_hi[:, slot % SPLIT, 0:kts, :], raw[:, slot % RAW, 0:kts, :], ACT.Copy)\
                    .then_inc(hi_ready, 1)

            def raw_uses(s, slot):
                return 16 // RAW * (s - slot % RAW) + 16

            def turn_hi(n, dst, k0, gain=None):
                for a in range(2):
                    act.wait_ge(turned, 2 * n + a + 1)
                    if gain is None:
                        last = act.activation(dst[:, bass.ds(k0 + 2 * a, 2), 0, :],
                                              tr[a][:, :].rearrange("p (k s) -> p k s", k=2), ACT.Copy)
                    else:
                        for i in range(2):
                            last = act.activation(dst[:, k0 + 2 * a + i, 0, :], tr[a][:, of(i, S)],
                                                  ACT.Copy, scale=gains[:, gain, bass.ds(k0 + 2 * a + i, 1)])
                    last.then_inc(turned_hi, 1)

            def squares(n, b):
                for t in range(T):
                    act.activation((ps_o, ps_s)[t][:, :], res[:, t, of(b)], ACT.Square,
                                   accum_out=sums[:, n, t, bass.ds(b, 1)]).then_inc(squares_ready, 1)

            def stage(layer, number, j, g):
                n = layer * NH + g * HEADS_G + j
                if number == 0:
                    act.wait_ge(qk_turned, n + 1)
                    act.activation(qkT[:, :, :].rearrange("p a s -> p (a s)"), tr[0][:, :], ACT.Copy)\
                        .then_inc(qk_copied, 1)
                elif number == 1 and layer == 0:
                    act.wait_ge(max_negated, n + 1)
                    for t, (a, b) in enumerate(((0, P), (P, 3 * P))):
                        last = act.activation(work1[:, a:b], work0[:, a:b], ACT.Exp, bias=neg_max[:, t:t + 1],
                                              accum_out=row_sum[:, t:t + 1])
                    last.then_inc(exp_ready, 1)
                elif number == 1:
                    act.wait_ge(scored, n + 1)
                    act.activation(work0[:, :], ps_z[j % 2][:, 0:3 * P], ACT.Abs).then_inc(shifted, 1)
                    act.wait_ge(shifted, n + 1)
                    act.activation(work1[:, :], work0[:, :], ACT.Exp, scale=-1.0).then_inc(exp_ready, 1)
                    act.wait_ge(exp_ready, n + 1)
                    act.activation(work0[:, :], work1[:, :], ACT.Ln, bias=1.0).then_inc(log_ready, 1)
                elif number == 2:
                    act.wait_ge(probs_turned, n + 1)
                    if layer == 0:
                        act.activation(probsT[:, :], tr[1][:, 0:3 * P], ACT.Copy).then_inc(probsT_ready, 1)
                    else:
                        act.activation(probsT[:, :], ps_z[j % 2][:, 0:3 * P], ACT.Exp).then_inc(probsT_ready, 1)
                elif number == 3:
                    act.wait_ge(head_summed, n + 1)
                    act.activation(oT[:, g * HEADS_G + j, 0, :], ps_o[:, 0:S], ACT.Copy).then_inc(head_hi, 1)

            def await_down(layer, b):
                act.wait_ge(acc_free, 2 * (layer * BLOCKS + BLOCKS - ND + b + 1))
                act.wait_ge(squares_ready, ((2 + 2 * layer) * ND + b) * T)

            def down_residual(layer, b):
                squares(2 + 2 * layer, b)
                if layer == 0:
                    for t in range(T):
                        copy = act.activation(mix[:, t, :], res[:, t, of(b)], ACT.Copy)
                    copy.then_inc(res_copied, 1)

            act.dma_start(attn_rows[:, :], attn_norm.rearrange("a (k p) -> (a k) p", p=P)).then_inc(attn_loaded, 16)
            act.preload_act_table_set("natural_log_exp_and_others")
            act.dma_start(gain_rows[0:2 * KD, :], ffn_norm.rearrange("a (k p) -> (a k) p", p=P)).then_inc(gains_loaded, 16)
            act.dma_start(gain_rows[2 * KD:3 * KD, :], kv_norm.rearrange("(k p) -> k p", p=P)).then_inc(gains_loaded, 16)
            act.dma_start(f_raw[:, :, :], win_t[:, :, 3 * D:3 * D + NH]).then_inc(f_loaded, 16)
            act.dma_start(f_bias[:, :], a_b_f[0].partition_broadcast(P)).then_inc(bias_loaded, 16)
            act.wait_ge(gains_turned, 1)
            act.activation(gains[:, 0:2, :].rearrange("p a k -> p (a k)"), tr[0][:, 0:2 * KD], ACT.Copy)\
                .then_inc(gains_ready, 1)
            act.wait_ge(gains_ready, 1)
            turn_hi(0, xT, 0, ATTN[0])
            split_hi(0, 0)
            turn_hi(1, xT, KT, ATTN[0])
            split_hi(1, 1)
            act.wait_ge(f_loaded, 16)
            act.activation(f_w[:, :, 0, :], f_raw[:, :, :], ACT.Copy).then_inc(f_split_hi, 1)
            act.wait_ge(gains_turned, 2)
            act.activation(gains[:, 2:5, :].rearrange("p a k -> p (a k)"), ps_o[:, 0:3 * KD], ACT.Copy)\
                .then_inc(gains_ready, 1)

            def qkv_group(layer, g, first):
                for step in range(QKV_STEPS):
                    s = layer * STEPS + g * QKV_STEPS + step
                    if first and layer == 1 and step == 0:
                        await_down(0, ND - 1)
                    split_hi(s + AHEAD, step + AHEAD)
                    if first and layer == 1 and step == 0:
                        down_residual(0, ND - 1)
                    if first and layer == 0 and step < 2:
                        turn_hi(2 + step, xT, (2 + step) * KT, ATTN[0])
                    if first and layer == 0 and 1 <= step <= 2:
                        for b in (2 * step - 2, 2 * step - 1):
                            for t in range(T):
                                if b + t > 0:
                                    act.wait_ge(squares_ready, b * T + t)
                                act.activation(ps_o[:, :], res[:, t, cols(b)], ACT.Square,
                                               accum_out=sums[:, 0, t, b:b + 1]).then_inc(squares_ready, 1)
                    if first and layer == 1 and step == 1:
                        turn_hi(TJ_DOWN + ND - 1, xT, (ND - 1) * KT, KV)
                    if first and layer == 1 and 2 <= step < 2 + KG:
                        turn_hi(TJ_Q + step - 2, xqT, (step - 2) * KT, ATTN[1])
                    if first and layer == 0 and step == KG:
                        act.wait_ge(f_step, 2)
                        act.activation(f_abs[:, :, :], f_logit[:, :, :], ACT.Abs).then_inc(f_act, 1)
                        act.wait_ge(f_act, 1)
                        act.activation(f_exp[:, :, :], f_abs[:, :, :], ACT.Exp, scale=-1.0).then_inc(f_act, 1)
                        act.wait_ge(f_act, 2)
                        act.activation(f_log1p[:, :, :], f_exp[:, :, :], ACT.Ln, bias=1.0).then_inc(f_act, 1)
                    for number, j, back in stages(step):
                        if not (first and back):
                            stage(layer, number, j, g - back)

            for layer in range(2):
                if layer == 1:
                    act.preload_act_table_set("natural_log_exp_and_others")
                qkv_group(layer, 0, True)
                with act.Fori(1, NG) as g:
                    qkv_group(layer, g, False)

                for i, (b, k) in enumerate(OUT_ORDER):
                    s = layer * STEPS + at_out + i
                    split_hi(s + AHEAD, i + AHEAD)
                    for number, j, back in stages(i):
                        if back:
                            stage(layer, number, j, NG - 1)
                    if k == KG - 1:
                        act.wait_ge(acc_free, 2 * (layer * BLOCKS + 3 * NG + b + 1))
                        act.wait_ge(squares_ready, ((1 + 2 * layer) * ND + b) * T)
                        squares(1 + 2 * layer, b)
                    turn = OUT_TURNS.get(i)
                    if turn is not None:
                        turn_hi(TJ_OUT[layer] + turn, xT, turn * KT, FFN[layer])

                def ffn_block(j, first):
                    for step in range(2 * KG):
                        s = layer * STEPS + at_ffn + j * 2 * KG + step
                        blk = layer * BLOCKS + 3 * NG + ND + 2 * j
                        if step == KG - 1:
                            if first:
                                act.wait_ge(rstd_ready, 2 + 2 * layer)
                            for t in range(T):
                                if t == 0:
                                    act.wait_ge(acc0_ready, blk + 1)
                                else:
                                    act.wait_ge(slab_done, s + 1)
                                act.activation(mix[:, t, :], acc[(1 + layer) % 2][t][:, :], ACT.Sigmoid,
                                               scale=rstd[:, 1 + 2 * layer, t:t + 1]).then_inc(sig_ready, 1)
                        split_hi(s + AHEAD, step + AHEAD)
                        if step == 1:
                            if first:
                                turn_hi(TJ_OUT[layer] + ND - 1, xT, (ND - 1) * KT, FFN[layer])
                            else:
                                turn_hi(TJ_FFN[layer] + j - 1, hid, (j - 1) * KT)

                ffn_block(0, True)
                with act.Fori(1, NF) as j:
                    ffn_block(j, False)

                def down_block(b, first=False, last=False):
                    for step in range(len(DOWN)):
                        s = layer * STEPS + at_down + b * len(DOWN) + step
                        if step == 0 and not first:
                            await_down(layer, b - 1)
                        if not (last and step + AHEAD >= len(DOWN)):
                            split_hi(s + AHEAD, step + AHEAD, DOWN[(step + AHEAD) % len(DOWN)])
                        if step == 1 and first:
                            turn_hi(TJ_FFN[layer] + NF - 1, hid, (NF - 1) * KT)
                        elif step == 1 and layer == 0:
                            turn_hi(TJ_DOWN + b - 1, xT, (b - 1) * KT, KV)
                        if step == 0 and not first:
                            down_residual(layer, b - 1)

                down_block(0, first=True)
                if layer == 0:
                    with act.Fori(1, ND) as b:
                        down_block(b)
                else:
                    with act.Fori(1, ND - 1) as b:
                        down_block(b)
                    down_block(ND - 1, last=True)
                    await_down(1, ND - 1)
                    down_residual(1, ND - 1)

        @block.vector
        def _(dve):
            def split_lo(s, slot, kts=KT):
                dve.wait_ge(hi_ready, s + 1)
                dve.tensor_tensor(w_lo[:, slot % SPLIT, 0:kts, :], raw[:, slot % RAW, 0:kts, :],
                                  w_hi[:, slot % SPLIT, 0:kts, :].bitcast(F32), ALU.subtract)\
                    .then_inc(lo_ready, 1)

            def turn_lo(n, dst, k0, gain=None):
                for a in range(2):
                    dve.wait_ge(turned_hi, 2 * n + a + 1)
                    if gain is None:
                        last = dve.tensor_tensor(dst[:, bass.ds(k0 + 2 * a, 2), 1, :],
                                                 tr[a][:, :].rearrange("p (k s) -> p k s", k=2),
                                                 dst[:, bass.ds(k0 + 2 * a, 2), 0, :].bitcast(F32), ALU.subtract)
                    else:
                        for i in range(2):
                            k = k0 + 2 * a + i
                            last = dve.scalar_tensor_tensor(
                                out=dst[:, k, 1, :], in0=tr[a][:, of(i, S)], scalar=gains[:, gain, bass.ds(k, 1)],
                                in1=dst[:, k, 0, :].bitcast(F32), op0=ALU.mult, op1=ALU.subtract)
                    last.then_inc(turned_lo, 1)

            def tile_summed(t, blk, s):
                if t == 0:
                    dve.wait_ge(acc0_ready, blk + 1)
                else:
                    dve.wait_ge(slab_done, s + 1)

            def take_qkv(layer, kind, blk, s, bank):
                for t in range(T):
                    tile_summed(t, blk, s)
                    dst = {"q": mix, "k": kn, "v": vn}[kind]
                    dve.tensor_scalar(dst[:, t, :], bank[t][:, :], rstd[:, 2 * layer, t:t + 1],
                                      SCALE if kind == "q" else None, ALU.mult,
                                      *([ALU.mult] if kind == "q" else [])).then_inc(acc_free, 1)

            def take_residual(b, blk, s, bank):
                for t in range(T):
                    tile_summed(t, blk, s)
                    dve.tensor_tensor(res[:, t, of(b)], res[:, t, of(b)], bank[t][:, :], ALU.add)\
                        .then_inc(acc_free, 1)

            def apply_gain(b):
                dve.wait_ge(squares_ready, (4 * ND + b + 1) * T)
                dve.wait_ge(gain_loaded, 16)
                for t in range(T):
                    dve.tensor_tensor(res[:, t, of(b)], res[:, t, of(b)], final_gain[:, of(b)], ALU.mult)\
                        .then_inc(gained, 1)

            def early(layer, number, j, g):
                n = layer * NH + g * HEADS_G + j
                h = g * HEADS_G + j
                if number == 1 and layer == 0:
                    dve.wait_ge(scored, n + 1)
                    for t, (a, b) in enumerate(((0, P), (P, 3 * P))):
                        last = dve.scalar_tensor_tensor(
                            out=work0[:, a:b], in0=ps_s[:, a:b], scalar=c_tok[:, t, bass.ds(h, 1)],
                            in1=neg_c[:, h, 0:b - a], op0=ALU.add, op1=ALU.add)
                    last.then_inc(shifted, 1)
                    dve.wait_ge(shifted, n + 1)
                    for t, (a, b) in enumerate(((0, P), (P, 3 * P))):
                        last = dve.tensor_reduce(row_max[:, t:t + 1], work0[:, a:b], AX_X, ALU.max)
                    last.then_inc(max_found, 1)
                    dve.wait_ge(max_found, n + 1)
                    dve.tensor_scalar(neg_max[:, :], row_max[:, :], -1.0, None, ALU.mult)\
                        .then_inc(max_negated, 1)

            def late(layer, number, j, g):
                n = layer * NH + g * HEADS_G + j
                if number == 1 and layer == 0:
                    dve.wait_ge(exp_ready, n + 1)
                    dve.reciprocal(row_inv[:, :], row_sum[:, :]).then_inc(inv_ready, 1)
                    dve.wait_ge(inv_ready, n + 1)
                    for t, (a, b) in enumerate(((0, P), (P, 3 * P))):
                        last = dve.tensor_scalar(work1[:, a:b], work1[:, a:b], row_inv[:, t:t + 1], None, ALU.mult)
                    last.then_inc(probs_ready, 1)
                elif number == 1:
                    dve.wait_ge(log_ready, n - NH + 1)
                    dve.scalar_tensor_tensor(out=work1[:, :], in0=ps_z[j % 2][:, 0:3 * P], scalar=0.0,
                                             in1=work0[:, :], op0=ALU.max, op1=ALU.add).then_inc(probs_ready, 1)
                elif number == 3:
                    dve.wait_ge(head_hi, n + 1)
                    dve.tensor_tensor(oT[:, g * HEADS_G + j, 1, :], ps_o[:, 0:S],
                                      oT[:, g * HEADS_G + j, 0, :].bitcast(F32), ALU.subtract)\
                        .then_inc(head_ready, 1)

            dve.wait_ge(gains_ready, 1)
            turn_lo(0, xT, 0, ATTN[0])
            split_lo(0, 0)
            turn_lo(1, xT, KT, ATTN[0])
            split_lo(1, 1)
            dve.wait_ge(f_split_hi, 1)
            dve.tensor_tensor(f_w[:, :, 1, :], f_raw[:, :, :], f_w[:, :, 0, :].bitcast(F32), ALU.subtract)\
                .then_inc(f_split_lo, 1)

            def qkv_group(layer, g, first):
                for step in range(QKV_STEPS):
                    s = layer * STEPS + g * QKV_STEPS + step
                    which = step // KG
                    if step % KG == KG - 1:
                        if first and step == KG - 1:
                            dve.wait_ge(rstd_ready, 1 + 2 * layer)
                        take_qkv(layer, QKV_KINDS[layer][which], layer * BLOCKS + 3 * g + which, s,
                                 acc[(which + layer) % 2])
                    if first and layer == 0 and step == KG:
                        dve.wait_ge(f_summed, 1)
                        dve.wait_ge(bias_loaded, 16)
                        for part, dst, add in ((0, f_part, None), (1, f_logit, f_part)):
                            if part == 1:
                                dve.wait_ge(f_step, 1)
                            for t in range(T):
                                at = (2 * t + part) * NH
                                mine = dve.scalar_tensor_tensor(
                                    out=dst[:, t, :], in0=ps_s[:, at:at + NH], scalar=rstd[:, 0, t:t + 1],
                                    in1=f_bias[:, :] if add is None else add[:, t, :],
                                    op0=ALU.mult, op1=ALU.add)
                            mine.then_inc(f_step, 1)
                    if first and layer == 0 and step == KG + 2:
                        dve.wait_ge(c_summed, 1)
                        dve.tensor_scalar(c_tok[:, :, :].rearrange("p t h -> p (t h)"), ps_s[:, 0:T * NH],
                                          -1.0, None, ALU.mult).then_inc(c_copied, 1)
                        dve.tensor_copy(c_row[:, :], ps_o[0:NH, 0:S]).then_inc(c_copied, 1)
                    if first and layer == 0 and step == FIRST_STAGE + 1:
                        dve.wait_ge(neg_c_loaded, 16)
                        dve.wait_ge(c_copied, 2)
                    todo = [(number, j, back) for number, j, back in stages(step) if not (first and back)]
                    for number, j, back in todo:
                        early(layer, number, j, g - back)
                    split_lo(s + AHEAD, step + AHEAD)
                    if first and layer == 0 and step < 2:
                        turn_lo(2 + step, xT, (2 + step) * KT, ATTN[0])
                    if first and layer == 1 and step == 1:
                        turn_lo(TJ_DOWN + ND - 1, xT, (ND - 1) * KT, KV)
                    if first and layer == 1 and 2 <= step < 2 + KG:
                        turn_lo(TJ_Q + step - 2, xqT, (step - 2) * KT, ATTN[1])
                    if first and layer == 0 and step == KG:
                        dve.wait_ge(f_act, 3)
                        dve.scalar_tensor_tensor(out=log_f[:, :, :], in0=f_logit[:, :, :], scalar=0.0,
                                                 in1=f_log1p[:, :, :], op0=ALU.min, op1=ALU.subtract)\
                            .then_inc(f_step, 1)
                    for number, j, back in todo:
                        late(layer, number, j, g - back)

            for layer in range(2):
                qkv_group(layer, 0, True)
                with dve.Fori(1, NG) as g:
                    qkv_group(layer, g, False)

                for i, (b, k) in enumerate(OUT_ORDER):
                    s = layer * STEPS + at_out + i
                    if k == KG - 1:
                        take_residual(b, layer * BLOCKS + 3 * NG + b, s, acc[(1 + b + layer) % 2])
                    todo = [(number, j) for number, j, back in stages(i) if back]
                    for number, j in todo:
                        early(layer, number, j, NG - 1)
                    split_lo(s + AHEAD, i + AHEAD)
                    for number, j in todo:
                        late(layer, number, j, NG - 1)
                    turn = OUT_TURNS.get(i)
                    if turn is not None:
                        turn_lo(TJ_OUT[layer] + turn, xT, turn * KT, FFN[layer])

                def ffn_block(j, first):
                    for step in range(2 * KG):
                        s = layer * STEPS + at_ffn + j * 2 * KG + step
                        blk = layer * BLOCKS + 3 * NG + ND + 2 * j
                        if step == KG - 1:
                            if first:
                                dve.wait_ge(rstd_ready, 2 + 2 * layer)
                            for t in range(T):
                                dve.wait_ge(sig_ready, T * (layer * NF + j) + t + 1)
                                dve.scalar_tensor_tensor(
                                    out=mix[:, t, :], in0=acc[(1 + layer) % 2][t][:, :],
                                    scalar=rstd[:, 1 + 2 * layer, t:t + 1], in1=mix[:, t, :],
                                    op0=ALU.mult, op1=ALU.mult).then_inc(acc_free, 1)
                        if step == 2 * KG - 1:
                            dve.wait_ge(acc_free, 2 * (blk + 1))
                            for t in range(T):
                                tile_summed(t, blk + 1, s)
                                dve.scalar_tensor_tensor(
                                    out=mix[:, t, :], in0=acc[layer % 2][t][:, :],
                                    scalar=rstd[:, 1 + 2 * layer, t:t + 1], in1=mix[:, t, :],
                                    op0=ALU.mult, op1=ALU.mult).then_inc(acc_free, 1)
                        split_lo(s + AHEAD, step + AHEAD)
                        if step == 1:
                            if first:
                                turn_lo(TJ_OUT[layer] + ND - 1, xT, (ND - 1) * KT, FFN[layer])
                            else:
                                turn_lo(TJ_FFN[layer] + j - 1, hid, (j - 1) * KT)

                ffn_block(0, True)
                with dve.Fori(1, NF) as j:
                    ffn_block(j, False)

                def down_block(b, first=False, last=False):
                    for step in range(len(DOWN)):
                        s = layer * STEPS + at_down + b * len(DOWN) + step
                        if step == len(DOWN) - 1:
                            take_residual(b, layer * BLOCKS + BLOCKS - ND + b, s,
                                          acc[(1 + layer) % 2 if first else layer % 2])
                        if not (last and step + AHEAD >= len(DOWN)):
                            split_lo(s + AHEAD, step + AHEAD, DOWN[(step + AHEAD) % len(DOWN)])
                        if step == 1 and first:
                            turn_lo(TJ_FFN[layer] + NF - 1, hid, (NF - 1) * KT)
                        elif step == 1 and layer == 0:
                            turn_lo(TJ_DOWN + b - 1, xT, (b - 1) * KT, KV)
                        elif step == 1:
                            apply_gain(b - 1)

                down_block(0, first=True)
                if layer == 0:
                    with dve.Fori(1, ND) as b:
                        down_block(b)
                else:
                    with dve.Fori(1, ND - 1) as b:
                        down_block(b)
                    down_block(ND - 1, last=True)

            apply_gain(ND - 1)
            dve.wait_ge(rstd_ready, 5)
            dve.wait_ge(gained, T * ND)
            for b in range(ND):
                for t in range(T):
                    dve.tensor_scalar(res[:, t, cols(b)], res[:, t, cols(b)], rstd[:, 4, t:t + 1], None,
                                      ALU.mult).then_inc(out_ready, 1)

        @block.tensor
        def _(pe):
            def slab(s, slot, kts, stat, k0, bank, first, last, blk, back=2, gates=None):
                pe.wait_ge(lo_ready, s + 1)
                for t in range(T):
                    if first and not (isinstance(blk, int) and blk < back):
                        pe.wait_ge(acc_free, 2 * (blk - back) + t + 1)
                    for k in range(kts):
                        for part, w in ((0, w_hi), (0, w_lo), (1, w_hi)):
                            mm = pe.matmul(bank[t][:, :], stat[:, k0 + k, part, t * P:(t + 1) * P],
                                           w[:, slot % SPLIT, k, :],
                                           start=(first and k == 0 and part == 0 and w is w_hi),
                                           stop=(last and k == kts - 1 and part == 1))
                            if gates is not None and w is w_hi:
                                kt, at = gates * KT + k, 2 * t * NH
                                gate = pe.matmul(ps_s[:, at:at + (2 - part) * NH],
                                                 xT[:, kt, part, t * P:(t + 1) * P],
                                                 f_w[:, kt, 0:2 - part, :].rearrange("p a h -> p (a h)"),
                                                 start=(kt == 0 and t == 0 and part == 0),
                                                 stop=(kt == KD - 1 and t == T - 1 and part == 1),
                                                 skip_group_check=True)
                    if t == 0 and last:
                        mm.then_inc(acc0_ready, 1)
                mm.then_inc(slab_done, 1)
                if gates == KG - 1:
                    gate.then_inc(f_summed, 1)

            def turn(n, src, b):
                for a in range(2):
                    if n_past_first(n):
                        pe.wait_ge(turned_lo, 2 * n + a - 1)
                    for i in range(2):
                        for t in range(T):
                            mm = pe.transpose(tr[a][:, i * S + t * P:i * S + (t + 1) * P],
                                              src(t, b, 2 * a + i), ident[:, :])
                    mm.then_inc(turned, 1)

            def n_past_first(n):
                return not (isinstance(n, int) and n == 0)

            def from_res(t, b, i):
                return res[:, t, b * COLS + i * P:b * COLS + (i + 1) * P]

            def from_mix(t, b, i):
                return mix[:, t, i * P:(i + 1) * P]

            def stage(layer, number, j, g):
                n = layer * NH + g * HEADS_G + j
                head = slice(j * DH, (j + 1) * DH)
                if number == 0:
                    if j == 0:
                        pe.wait_ge(acc_free, 2 * (layer * BLOCKS + 3 * g + 2))
                    for a, src in enumerate((mix, kn)):
                        for t in range(T):
                            mm = pe.transpose(tr[0][:, a * S + t * P:a * S + (t + 1) * P],
                                              src[:, t, head], ident[:, :])
                    mm.then_inc(qk_turned, 1)
                elif number == 1 and layer == 0:
                    pe.wait_ge(qk_copied, n + 1)
                    for t, (a, b) in enumerate(((0, P), (P, 3 * P))):
                        pe.matmul(ps_s[:, a:b], qkT[:, 0, t * P:(t + 1) * P], qkT[:, 1, 0:b - a],
                                  start=True, stop=False)
                        mm = pe.matmul(ps_s[:, b - P:b], ident_b[:, :], mask_q[:, :], start=False, stop=True)
                    mm.then_inc(scored, 1)
                elif number == 1:
                    z = ps_z[j % 2]
                    pe.wait_ge(qk_copied, n + 1)
                    pe.matmul(z[:, 0:S], qkT[:, 1, 0:P], qkT[:, 0, 0:S], start=True, stop=False,
                              skip_group_check=True)
                    pe.matmul(z[:, 0:P], ident_b[:, :], mask_k[:, :], start=False, stop=False,
                              skip_group_check=True)
                    pe.matmul(z[:, S:S + P], qkT[:, 1, P:S], qkT[:, 0, P:S], start=False, stop=False,
                              skip_group_check=True)
                    mm = pe.matmul(z[:, S:S + P], ident_b[:, :], mask_k[:, :], start=False, stop=True,
                                   skip_group_check=True)
                    mm.then_inc(scored, 1)
                elif number == 2 and layer == 0:
                    pe.wait_ge(probs_ready, n + 1)
                    for i in range(3):
                        mm = pe.transpose(tr[1][:, i * P:(i + 1) * P], work1[:, i * P:(i + 1) * P], ident[:, :])
                    mm.then_inc(probs_turned, 1)
                elif number == 2:
                    z = ps_z[j % 2]
                    pe.wait_ge(probs_ready, n + 1)
                    pe.matmul(z[:, 0:S], neg_suffix[:, :], work1[:, 0:S], start=False, stop=False,
                              skip_group_check=True)
                    pe.matmul(z[:, P:S], neg_ones[:, :], work1[:, S:S + P], start=False, stop=False,
                              skip_group_check=True)
                    mm = pe.matmul(z[:, S:S + P], neg_suffix[:, :], work1[:, S:S + P], start=False, stop=True,
                                   skip_group_check=True)
                    mm.then_inc(probs_turned, 1)
                else:
                    if j == 0:
                        pe.wait_ge(acc_free, 2 * (layer * BLOCKS + 3 * g + 3))
                    if not (isinstance(n, int) and n == 0):
                        pe.wait_ge(head_ready, n)
                    pe.wait_ge(probsT_ready, n + 1)
                    pe.matmul(ps_o[:, 0:S], vn[:, 0, head], probsT[:, 0:S], start=True, stop=False)
                    mm = pe.matmul(ps_o[:, P:S], vn[:, 1, head], probsT[:, S:S + P], start=False, stop=True)
                    mm.then_inc(head_summed, 1)

            pe.wait_ge(ident_ready, 1)
            pe.wait_ge(attn_loaded, 16)
            pe.transpose(tr[0][:, 0:2 * KD], attn_rows[:, :], ident[0:2 * KD, 0:2 * KD]).then_inc(gains_turned, 1)
            pe.wait_ge(gains_ready, 1)
            for b in range(2):
                pe.wait_ge(x_loaded[b], 16)
                turn(b, from_res, b)
            pe.wait_ge(gains_loaded, 16 * 2)
            pe.transpose(ps_o[:, 0:3 * KD], gain_rows[:, :], ident[0:3 * KD, 0:3 * KD]).then_inc(gains_turned, 1)

            def qkv_group(layer, g, first):
                for step in range(QKV_STEPS):
                    s = layer * STEPS + g * QKV_STEPS + step
                    which, k = divmod(step, KG)
                    kind = QKV_KINDS[layer][which]
                    stat = xqT if layer == 1 and kind == "q" else xT
                    if first and which == 0:
                        pe.wait_ge(turned_lo, 2 * ((TJ_DOWN if layer else 0) + k + 1))
                    if first and stat is xqT:
                        pe.wait_ge(turned_lo, 2 * (TJ_Q + k + 1))
                    slab(s, step, KT, stat, k * KT, acc[(which + layer) % 2], k == 0, k == KG - 1,
                         layer * BLOCKS + 3 * g + which, 1 if which == 0 and not first else 2,
                         step - 1 if first and layer == 0 and 1 <= step <= KG else None)
                    if first and layer == 0 and step < 2:
                        pe.wait_ge(x_loaded[2 + step], 16)
                        turn(2 + step, from_res, 2 + step)
                    if first and layer == 0 and step == 0:
                        pe.wait_ge(f_split_lo, 1)
                    if first and layer == 1 and step == 1:
                        pe.wait_ge(acc_free, 2 * BLOCKS)
                        turn(TJ_DOWN + ND - 1, from_res, ND - 1)
                    if first and layer == 1 and 2 <= step < 2 + KG:
                        turn(TJ_Q + step - 2, from_res, step - 2)
                    if first and layer == 0 and step == KG + 2:
                        pe.wait_ge(consts_ready, 5)
                        pe.wait_ge(f_step, 3)
                        pe.matmul(ps_s[:, 0:NH], neg_prefix[:, :], log_f[:, 0, :], start=True, stop=True)
                        pe.matmul(ps_s[:, NH:2 * NH], neg_ones[:, :], log_f[:, 0, :], start=True, stop=False)
                        pe.matmul(ps_s[:, NH:2 * NH], neg_prefix[:, :], log_f[:, 1, :], start=False, stop=True)
                        pe.matmul(ps_o[0:NH, 0:P], log_f[:, 0, :], neg_prefix[:, :], start=True, stop=True)
                        pe.matmul(ps_o[0:NH, P:S], log_f[:, 0, :], neg_ones[:, :], start=True, stop=False)
                        mm = pe.matmul(ps_o[0:NH, P:S], log_f[:, 1, :], neg_prefix[:, :], start=False, stop=True)
                        mm.then_inc(c_summed, 1)
                    if first and layer == 0 and step == FIRST_STAGE:
                        pe.wait_ge(c_copied, 2)
                    for number, j, back in stages(step):
                        if not (first and back):
                            stage(layer, number, j, g - back)

            for layer in range(2):
                qkv_group(layer, 0, True)
                with pe.Fori(1, NG) as g:
                    qkv_group(layer, g, False)

                for i, (b, k) in enumerate(OUT_ORDER):
                    pe.wait_ge(head_ready, layer * NH + HEADS_G * (k + 1))
                    slab(layer * STEPS + at_out + i, i, KT, oT, k * KT, acc[(1 + b + layer) % 2], k == 0,
                         k == KG - 1, layer * BLOCKS + 3 * NG + b)
                    for number, j, back in stages(i):
                        if back:
                            stage(layer, number, j, NG - 1)
                    t = OUT_TURNS.get(i)
                    if t is not None:
                        pe.wait_ge(acc_free, 2 * (layer * BLOCKS + 3 * NG + t + 1))
                        turn(TJ_OUT[layer] + t, from_res, t)

                def ffn_block(j, first):
                    for step in range(2 * KG):
                        which, k = divmod(step, KG)
                        blk = layer * BLOCKS + 3 * NG + ND + 2 * j
                        if first and which == 0:
                            pe.wait_ge(turned_lo, 2 * (TJ_OUT[layer] + k + 1))
                        slab(layer * STEPS + at_ffn + j * 2 * KG + step, step, KT, xT, k * KT,
                             acc[(1 + which + layer) % 2], k == 0, k == KG - 1, blk + which)
                        if step == 1:
                            pe.wait_ge(acc_free, 2 * blk)
                            if first:
                                turn(TJ_OUT[layer] + ND - 1, from_res, ND - 1)
                            else:
                                turn(TJ_FFN[layer] + j - 1, from_mix, 0)

                ffn_block(0, True)
                with pe.Fori(1, NF) as j:
                    ffn_block(j, False)

                def down_block(b, first=False):
                    k0 = 0
                    blk = layer * BLOCKS + BLOCKS - ND + b
                    for step, kts in enumerate(DOWN):
                        if first:
                            pe.wait_ge(turned_lo, 2 * (TJ_FFN[layer] + (k0 + kts - 1) // KT + 1))
                        slab(layer * STEPS + at_down + b * len(DOWN) + step, step, kts, hid, k0,
                             acc[(1 + layer) % 2 if first else layer % 2], step == 0, step == len(DOWN) - 1,
                             blk, 2 if first else 1)
                        k0 += kts
                        if step == 1 and first:
                            pe.wait_ge(acc_free, 2 * blk)
                            turn(TJ_FFN[layer] + NF - 1, from_mix, 0)
                        elif step == 1 and layer == 0:
                            pe.wait_ge(res_copied, b)
                            turn(TJ_DOWN + b - 1, from_mix, 0)

                down_block(0, first=True)
                with pe.Fori(1, ND) as b:
                    down_block(b)


OUT_TURNS = {8: 0, 9: 1, 13: 2}


_INS = ["x", "attn_norm", "ffn_norm", "a_w_in", "a_b_f", "a_w_out", "kv_norm", "w_kv", "b_w_q", "b_w_out",
        "ffn_w_gate", "ffn_w_up", "ffn_w_down", "final_norm"]


def kernel(**inputs):
    import numpy as _np
    import concourse.bacc as _bacc
    from concourse import mybir as _mybir
    from concourse.bass_utils import run_bass_kernel_spmd as _run

    nc = _bacc.Bacc("TRN2", target_bir_lowering=False, num_devices=1)
    arrays, args = {}, []
    for name in _INS:
        a = _np.ascontiguousarray(inputs[name])
        arrays[f"in_{name}_dram"] = a
        args.append(nc.dram_tensor(f"in_{name}_dram", a.shape, _mybir.dt.from_np(a.dtype), kind="ExternalInput").ap())
    shape = inputs["x"].shape
    args.append(nc.dram_tensor("out_0_dram", shape, _mybir.dt.float32, kind="ExternalOutput").ap())
    build(nc, *args)
    r = _run(nc, [arrays], core_ids=[0])
    return r.results[0]["out_0_dram"]
```
